# Optimizing a Trainium2 kernel written in Bass

```python
import jax, jax.numpy as jnp
from jax import lax
import numpy as np

D_MODEL = 1024
BATCH = 1
SEQ = 1024
DEPTH = 1

D_MIX = D_MODEL
HEAD_DIM = 64
ATT_WIDTH = D_MIX // 2
ATT_Q_HEADS = ATT_WIDTH // HEAD_DIM
ATT_KV_HEADS = 2
ATT_GROUP = ATT_Q_HEADS // ATT_KV_HEADS
ATT_KV_WIDTH = ATT_KV_HEADS * HEAD_DIM
Q_BLOCK = 128
ROPE_THETA = 10000.0
GRID_W = 64
RWKV_WIDTH = D_MIX - ATT_WIDTH
RWKV_HEADS = RWKV_WIDTH // HEAD_DIM
DECAY_RANK = 64
ICLR_RANK = 64
N_DIRS = 2
RWKV_SHIFT_WIDTH = 3 * RWKV_WIDTH + DECAY_RANK + ICLR_RANK
IN_SPLITS = (ATT_WIDTH, ATT_KV_WIDTH, ATT_KV_WIDTH, ATT_WIDTH, RWKV_SHIFT_WIDTH, RWKV_WIDTH)
IN_WIDTH = ATT_WIDTH + 2 * ATT_KV_WIDTH + ATT_WIDTH + RWKV_SHIFT_WIDTH + RWKV_WIDTH
DECAY_SCALE = 0.6065306597126334
NORM_EPS = 1e-6
GN_EPS = 64e-5
L2_EPS = 1e-12

kernel_name = "hybrid_gqa_rwkv7_parallel_heads"

def rms_norm(x, g, eps=NORM_EPS):
    xf = x.astype(jnp.float32)
    y = xf * lax.rsqrt(jnp.mean(xf * xf, axis=-1, keepdims=True) + eps)
    return (y * g.astype(jnp.float32)).astype(x.dtype)

def axial_rope_tables(T, dtype):
    rows = T // GRID_W
    row = jnp.repeat(jnp.arange(rows, dtype=jnp.float32), GRID_W)
    col = jnp.tile(jnp.arange(GRID_W, dtype=jnp.float32), rows)
    n_freq = HEAD_DIM // 4
    inv_freq = ROPE_THETA ** (-jnp.arange(n_freq, dtype=jnp.float32) / n_freq)
    ang_r = row[:, None, None] * inv_freq
    ang_c = col[:, None, None] * inv_freq
    return (jnp.cos(ang_r).astype(dtype), jnp.sin(ang_r).astype(dtype),
            jnp.cos(ang_c).astype(dtype), jnp.sin(ang_c).astype(dtype))

def rotate_axis(x, cos, sin):
    n = x.shape[-1] // 2
    x1, x2 = x[..., :n], x[..., n:]
    return jnp.concatenate([x1 * cos - x2 * sin, x2 * cos + x1 * sin], axis=-1)

def apply_axial_rope(x, tables):
    cos_r, sin_r, cos_c, sin_c = tables
    half = HEAD_DIM // 2
    return jnp.concatenate([rotate_axis(x[..., :half], cos_r, sin_r),
                            rotate_axis(x[..., half:], cos_c, sin_c)], axis=-1)

def axial_gqa_attention(q, k, v, q_norm_g, k_norm_g):
    B, T, _ = q.shape
    q = rms_norm(q.reshape(B, T, ATT_Q_HEADS, HEAD_DIM), q_norm_g)
    k = rms_norm(k.reshape(B, T, ATT_KV_HEADS, HEAD_DIM), k_norm_g)
    v = v.reshape(B, T, ATT_KV_HEADS, HEAD_DIM)
    tables = axial_rope_tables(T, q.dtype)
    q = apply_axial_rope(q, tables)
    k = apply_axial_rope(k, tables)
    n_blk = T // Q_BLOCK
    q_blocks = q.reshape(B, n_blk, Q_BLOCK, ATT_KV_HEADS, ATT_GROUP, HEAD_DIM).transpose(1, 0, 3, 4, 2, 5)
    k_t = k.transpose(0, 2, 1, 3)
    v_t = v.transpose(0, 2, 1, 3)
    scale = HEAD_DIM ** -0.5

    def attend(q_blk):
        s = jnp.einsum('bkgqd,bksd->bkgqs', q_blk, k_t).astype(jnp.float32) * scale
        p = jax.nn.softmax(s, axis=-1).astype(v_t.dtype)
        return jnp.einsum('bkgqs,bksd->bkgqd', p, v_t)

    o = lax.map(attend, q_blocks)
    return o.transpose(1, 0, 4, 2, 3, 5).reshape(B, T, ATT_WIDTH)

def centered_shift(x, taps):
    xp = jnp.pad(x, ((0, 0), (1, 1), (0, 0)))
    return taps[0] * xp[:, :-2] + taps[1] * xp[:, 1:-1] + taps[2] * xp[:, 2:]

def bidir_rwkv7(r, k, v, wd, ad, w_up, w0, a_up, a0, k_k, k_a, r_k, gn_w, gn_b):
    f32 = jnp.float32
    B, T, _ = r.shape
    H, N = RWKV_HEADS, HEAD_DIM
    rf, kf, vf = r.astype(f32), k.astype(f32), v.astype(f32)
    heads = lambda z: z.reshape(z.shape[:-1] + (H, N))
    w = jnp.exp(-DECAY_SCALE * jax.nn.sigmoid(
        w0.astype(f32)[:, None, None, :]
        + jnp.einsum('btr,zrc->zbtc', jnp.tanh(wd.astype(f32)), w_up.astype(f32))))
    a = jax.nn.sigmoid(a0.astype(f32)[:, None, None, :]
                       + jnp.einsum('btr,zrc->zbtc', ad.astype(f32), a_up.astype(f32)))
    kk = heads(kf * k_k.astype(f32))
    kk = kk * lax.rsqrt(jnp.sum(kk * kk, axis=-1, keepdims=True) + L2_EPS)
    kt = kf[None] * (1.0 + (a - 1.0) * k_a.astype(f32))
    akk = heads(a) * kk[None]

    both = lambda z: jnp.stack([z, z])

    def time_major(z):
        z = jnp.stack([z[0], jnp.flip(z[1], axis=1)])
        return jnp.moveaxis(z, 2, 0)

    xs = (time_major(heads(w)), time_major(heads(kt)), time_major(both(heads(vf))),
          time_major(both(heads(rf))), time_major(both(kk)), time_major(akk))
    S0 = jnp.zeros((N_DIRS, B, H, N, N), f32)

    def step(S, inp):
        w_t, k_t, v_t, r_t, kk_t, akk_t = inp
        S = (S * w_t[..., None, :]
             - jnp.einsum('zbhvk,zbhk->zbhv', S, kk_t)[..., None] * akk_t[..., None, :]
             + v_t[..., :, None] * k_t[..., None, :])
        return S, jnp.einsum('zbhvk,zbhk->zbhv', S, r_t)

    _, ys = lax.scan(step, S0, xs)
    ys = jnp.moveaxis(ys, 0, 2)
    y = ys[0] + jnp.flip(ys[1], axis=1)
    mu = jnp.mean(y, axis=-1, keepdims=True)
    var = jnp.mean((y - mu) ** 2, axis=-1, keepdims=True)
    y = (y - mu) * lax.rsqrt(var + GN_EPS) * heads(gn_w.astype(f32)) + heads(gn_b.astype(f32))
    bonus = jnp.einsum('bthn,zbthn,hn->bth', heads(rf), heads(kt), r_k.astype(f32))[..., None] * heads(vf)
    return (y + bonus).reshape(B, T, RWKV_WIDTH)

def setup_inputs(seed: int = 0) -> dict:
    key = jax.random.key(seed)
    ks = jax.random.split(key, 24)
    L, D = DEPTH, D_MODEL
    nrm = jax.random.normal
    x = nrm(ks[0], (BATCH, SEQ, D), jnp.float32)
    c = nrm(ks[1], (BATCH, D), jnp.float32)
    w_ada = nrm(ks[2], (L, D, 3 * D), jnp.float32) * D ** -0.5
    b_ada = 0.01 * nrm(ks[3], (L, 3 * D), jnp.float32)
    g_pre = 1.0 + 0.05 * nrm(ks[4], (L, D), jnp.float32)
    w_in = nrm(ks[5], (L, D, IN_WIDTH), jnp.float32) * D ** -0.5
    q_norm_g = 1.0 + 0.05 * nrm(ks[6], (L, HEAD_DIM), jnp.float32)
    k_norm_g = 1.0 + 0.05 * nrm(ks[7], (L, HEAD_DIM), jnp.float32)
    shift_taps = (jnp.array([0.25, 1.0, 0.25], jnp.float32)[None, :, None]
                  + 0.05 * nrm(ks[8], (L, 3, RWKV_SHIFT_WIDTH), jnp.float32))
    w_up = 0.1 * nrm(ks[9], (L, N_DIRS, DECAY_RANK, RWKV_WIDTH), jnp.float32)
    w0 = jax.random.uniform(ks[10], (L, N_DIRS, RWKV_WIDTH), jnp.float32, -3.0, 3.0)
    a_up = 0.1 * nrm(ks[11], (L, N_DIRS, ICLR_RANK, RWKV_WIDTH), jnp.float32)
    a0 = 0.5 * nrm(ks[12], (L, N_DIRS, RWKV_WIDTH), jnp.float32)
    k_k = 0.85 + 0.05 * nrm(ks[13], (L, RWKV_WIDTH), jnp.float32)
    k_a = 1.0 + 0.05 * nrm(ks[14], (L, RWKV_WIDTH), jnp.float32)
    r_k = 0.1 * nrm(ks[15], (L, RWKV_HEADS, HEAD_DIM), jnp.float32)
    gn_w = 1.0 + 0.05 * nrm(ks[16], (L, RWKV_WIDTH), jnp.float32)
    gn_b = 0.01 * nrm(ks[17], (L, RWKV_WIDTH), jnp.float32)
    w_out = nrm(ks[18], (L, D_MIX, D), jnp.float32) * D_MIX ** -0.5
    g_post = 1.0 + 0.05 * nrm(ks[19], (L, D), jnp.float32)
    return {"x": x, "c": c, "w_ada": w_ada, "b_ada": b_ada, "g_pre": g_pre, "w_in": w_in,
            "q_norm_g": q_norm_g, "k_norm_g": k_norm_g, "shift_taps": shift_taps,
            "w_up": w_up, "w0": w0, "a_up": a_up, "a0": a0, "k_k": k_k, "k_a": k_a,
            "r_k": r_k, "gn_w": gn_w, "gn_b": gn_b, "w_out": w_out, "g_post": g_post}

def reference(x, c, w_ada, b_ada, g_pre, w_in, q_norm_g, k_norm_g, shift_taps,
              w_up, w0, a_up, a0, k_k, k_a, r_k, gn_w, gn_b, w_out, g_post):
    split_idx = [int(i) for i in np.cumsum(IN_SPLITS)[:-1]]
    rwkv_idx = [RWKV_WIDTH, 2 * RWKV_WIDTH, 3 * RWKV_WIDTH, 3 * RWKV_WIDTH + DECAY_RANK]
    c_act = jax.nn.silu(c)
    for l in range(DEPTH):
        mod = jnp.einsum('bd,de->be', c_act, w_ada[l]) + b_ada[l]
        shift, scale, gate = jnp.split(mod, 3, axis=-1)
        h = rms_norm(x, g_pre[l]) * (1.0 + scale[:, None, :]) + shift[:, None, :]
        proj = jnp.einsum('btd,dp->btp', h, w_in[l])
        q, k, v, g_att, rwkv_in, g_rwkv = jnp.split(proj, split_idx, axis=-1)
        y_att = axial_gqa_attention(q, k, v, q_norm_g[l], k_norm_g[l])
        rwkv_in = centered_shift(rwkv_in, shift_taps[l])
        r, kr, vr, wd, ad = jnp.split(rwkv_in, rwkv_idx, axis=-1)
        y_rwkv = bidir_rwkv7(r, kr, vr, wd, ad, w_up[l], w0[l], a_up[l], a0[l],
                             k_k[l], k_a[l], r_k[l], gn_w[l], gn_b[l]).astype(x.dtype)
        mixed = jnp.concatenate([y_att * jax.nn.silu(g_att), y_rwkv * jax.nn.silu(g_rwkv)], axis=-1)
        out = jnp.einsum('btm,md->btd', mixed, w_out[l])
        x = x + gate[:, None, :] * rms_norm(out, g_post[l])
    return x


_drawn_inputs = setup_inputs


def setup_inputs(seed=0):
    import zlib

    import numpy as np

    out = dict(_drawn_inputs(seed))
    spreads = {}
    factors = {'b_ada': 3.77, 'q_norm_g': 8.0, 'k_norm_g': 8.0, 'k_k': 5.448, 'gn_w': 6.416, 'gn_b': 64.0}
    for name, (base, spread) in spreads.items():
        noise = np.random.default_rng([zlib.crc32(name.encode()), seed]).standard_normal(out[name].shape)
        drawn = base * np.exp(spread * noise) if base else spread * noise
        out[name] = __import__('jax').numpy.asarray(drawn.astype(out[name].dtype))
    for name, factor in factors.items():
        out[name] = (out[name] * factor).astype(out[name].dtype)
    return out
```

```python
import concourse.bass as bass
from concourse import mybir
from contextlib import ExitStack

F32 = mybir.dt.float32
F32R = mybir.dt.float32r
BF16 = mybir.dt.bfloat16
ALU = mybir.AluOpType
ACT = mybir.ActivationFunctionType
AXX = mybir.AxisListType.X
ds = bass.ds

P = 128
T = 1024
D = 1024
KD = D // P
TT = T // P
NH = 8
HD = 64
KVH = 2
PAIRS = NH * HD // P
STEPS = PAIRS * TT
RANK = 64
IN_W = 3456
SLOTS = IN_W // P
Q0, K0, V0, GA0, R0, RK0, RV0, WA0, GR0 = 0, 4, 5, 6, 10, 14, 18, 22, 23
ORDER = (slice(None), slice(None, None, -1))
NCONV = 13
DECAY = 0.6065306597126334
NORM_EPS, GN_EPS, L2_EPS = 1e-6, 64e-5, 1e-12
HALF = 512

PC = {}
_n = 0
for _name, _w in (("c", KD), ("b_shift", KD), ("b_scale", KD), ("g_pre", KD), ("taps", 3 * NCONV),
                  ("w0", 2 * PAIRS), ("a0", 2 * PAIRS), ("k_k", PAIRS), ("k_a", PAIRS), ("r_k", PAIRS),
                  ("gn_w", PAIRS), ("gn_b", PAIRS), ("q_g", 1), ("k_g", 1)):
    PC[_name] = _n
    _n += _w
NPC = _n

CC = {}
_n = 0
for _name, _w in (("ident", P), ("blocks", P), ("rot", P), ("rows", 9 * 32), ("mask", 4 * 2 * P), ("bd", P), ("keep", 4 * TT),
                  ("cos", T), ("sin", T), ("start", T), ("spread", 9 * P), ("eps", 1)):
    CC[_name] = _n
    _n += _w
NCC = _n


class Chain:

    def __init__(self, eng, sem, base=0):
        self.eng, self.sem, self.base, self.n = eng, sem, base, 0

    def sig(self, ins):
        self.n += 1
        ins.then_inc(self.sem, 1)
        return self.n

    def upto(self, n):
        self.eng.wait_ge(self.sem, self.base + n)

    def link(self, ins):
        self.upto(self.sig(ins))

    def next_block(self, steps=1):
        self.base = self.base + steps * self.n
        self.n = 0


def hybrid_layer(nc, x, w_ada, w_in, w_up, a_up, w_out, b_gate, g_post, params, consts, out):
    ctx = ExitStack()
    sb = lambda name, shape, dt=F32: ctx.enter_context(nc.sbuf_tensor(name, shape, dt))
    used = []

    def sem(name):
        used.append(nc.alloc_semaphore(name=name))
        return used[-1]

    def release_semaphores():
        nc.clear_and_free_semaphores(used)
        used.clear()
        nc.all_engine_barrier()

    PJ = sb("PJ", [P, SLOTS, T])
    HT = sb("HT", [P, KD, T])
    PRM = sb("PRM", [P, NPC])
    IDN = sb("IDN", [P, P])
    EMU = sb("EMU", [P, 2 * PAIRS * TT])
    CACT = sb("CACT", [P, KD])
    PS = ctx.enter_context(nc.psum_tensor("PS", [P, 8, HALF], F32))
    prm = lambda name, j=0: PRM[:, PC[name] + j:PC[name] + j + 1]

    with ctx:
        start_and_project(nc, sem, PJ, HT, PRM, IDN, CACT, PS, prm, x, w_ada, w_in, params, consts)
        units = nc.dram_tensor("units", (2, STEPS, P, 5, P), F32).ap()
        norm_and_rotate(nc, sem, PJ, HT, PRM, IDN, PS, prm, consts)
        prepare_units(nc, sem, PJ, HT, PRM, EMU, PS, prm, w_up, a_up, consts, units)
        WO7 = sb("WO7", [P, D])
        WO = [PJ[:, j, :] for j in (K0, V0, WA0, R0, R0 + 1, R0 + 2, R0 + 3)] + [WO7[:, :]]
        GACC = sb("GACC", [P, D])
        release_semaphores()
        views = [PJ[:, j:j + 4, :].rearrange("p (z a) b -> p z (a b)", z=2).rearrange("p z (g n) -> p z g n", n=32)
                 for j in (RK0, Q0)]
        INV = [[v[:, z] for z in range(2)] for v in views]
        key_products(nc, sem, PJ, PS, units)
        attend(nc, sem, PJ, PRM, IDN, PS, INV)
        release_semaphores()
        state_passes(nc, sem, PJ, HT, IDN, EMU, CACT, PS, consts, units, INV, WO, GACC, w_out, w_ada)
        finish_layer(nc, sem, PJ, HT, PRM, IDN, PS, prm, WO, GACC, x, b_gate, g_post, consts, out)
    return nc


def start_and_project(nc, sem, PJ, HT, PRM, IDN, CACT, PS, prm, x, w_ada, w_in, params, consts):
    with ExitStack() as st:
        sb = lambda name, shape, dt=F32: st.enter_context(nc.sbuf_tensor(name, shape, dt))
        WR = sb("WR", [P, 2, KD, P])
        ACC = sb("ACC", [P, 2 * D])
        ONES = sb("ONES", [P, 1])
        SS = sb("SS", [P, TT])
        RS = sb("RS", [P, TT])
        AM = sb("AM", [P, KD])
        BM = sb("BM", [P, KD])
        X = PJ[:, 0:8, :]
        WA = [PJ[:, 8 + 2 * u:10 + 2 * u, :].rearrange("p a b -> p (a b)") for u in range(8)]
        s_prm, s_x = sem("prm_loaded"), sem("x_loaded")
        s_wada = [sem(f"wada_loaded{k}") for k in range(KD)]
        s_w = [sem(f"w_loaded{u}") for u in range(2)]
        s_act, s_dve = sem("act_chain1"), sem("dve_chain1")
        s_cact, s_acc, s_mod, s_am = sem("c_act_ready"), sem("acc_ready"), sem("mod_summed"), sem("mod_ready")
        s_ss, s_rs, s_xn = sem("x_squares"), sem("x_rstd"), sem("x_normed")
        s_tr, s_shifted, s_copied = sem("x_transposed"), sem("shifted_tiles_plus_2"), sem("copied_tiles")
        s_ht = [sem("h_by_act"), sem("h_by_dve")]
        s_mm, s_tap = sem("proj_done_plus_2"), sem("centre_tap_done")

        win = lambda slot: w_in[:, ds(slot * P, P)].rearrange("(k p) n -> p k n", p=P)

        RUNS = [(R0, 6, (1, 1)), (WA0, 1, (1, 0)), (GR0 + 1, 1, (0, 0)), (0, 5, (0, 0))]
        LAST = GR0 + 3

        def pairs(eng, body, runs=RUNS):
            n0 = 0
            for run, (slot0, count, conv) in enumerate(runs):
                if count > 1:
                    with eng.Fori(0, count) as i:
                        for u in range(2):
                            body(n0 + 2 * i + u, slot0 + 2 * i + u, u, conv[u], n0 // 2 + i, run)
                else:
                    for u in range(2):
                        body(n0 + u, slot0 + u, u, conv[u], n0 // 2, run)
                n0 += 2 * count
            if runs is RUNS:
                body(n0, LAST, 0, 0, n0 // 2, len(RUNS))

        with nc.Block() as block:
            @block.sync
            def _(sp):
                sp.dma_start(PRM[:, :], params).then_inc(s_prm, 16)
                sp.dma_start(IDN[:, :], consts[:, CC["ident"]:CC["ident"] + P]).then_inc(s_prm, 16)
                for k in range(KD):
                    sp.dma_start(WA[k], w_ada[k * P:(k + 1) * P, 0:2 * D]).then_inc(s_wada[k], 16)
                sp.dma_start(X, x.rearrange("(t p) d -> p t d", p=P)).then_inc(s_x, 16)

                def load(n, slot, u, conv, k, run):
                    sp.wait_ge(s_mm, n + 1)
                    sp.dma_start(WR[:, u], win(slot)).then_inc(s_w[u], 16)
                pairs(sp, load)

            @block.gpsimd
            def _(pool):
                pool.memset(ONES[:, :], 1.0).then_inc(s_cact, 1)

            @block.scalar
            def _(act):
                chain = Chain(act, s_act)
                act.wait_ge(s_prm, 32)
                act.activation(CACT[:, :], PRM[:, PC["c"]:PC["c"] + KD], ACT.Tanh, scale=0.5).then_inc(s_cact, 1)
                act.wait_ge(s_x, 16)
                for t in range(TT):
                    act.activation(HT[:, t], X[:, t], ACT.Square, accum_out=SS[:, t:t + 1]).then_inc(s_ss, 1)
                act.wait_ge(s_rs, 1)
                act.activation(RS[:, :], SS[:, :], ACT.Sqrt).then_inc(s_rs, 1)
                act.wait_ge(s_rs, 2)
                for t in range(TT):
                    act.activation(X[:, t], X[:, t], ACT.Copy, scale=RS[:, t:t + 1]).then_inc(s_xn, 1)
                act.wait_ge(s_am, 2)
                for j in range(2 * KD):
                    if j % 2 == 0:
                        act.wait_ge(s_tr, j + 1)
                        act.activation(HT[:, j // 2, (j % 2) * HALF:(j % 2 + 1) * HALF], PS[:, j % 4], ACT.Identity,
                                       scale=AM[:, j // 2:j // 2 + 1], bias=BM[:, j // 2:j // 2 + 1]).then_inc(s_ht[0], 1)

                def evacuate(n, slot, u, conv, k, run):
                    act.wait_ge(s_mm, n + 3)
                    src = PS[:, 4 + 2 * u:6 + 2 * u].rearrange("p a b -> p (a b)")
                    dst = PJ[:, ds(slot, 1), :].rearrange("p a b -> p (a b)")
                    if conv:
                        tap = PRM[:, ds(PC["taps"] + NCONV + (slot - R0), 1)]
                        act.activation(dst, src, ACT.Copy, scale=tap).then_inc(s_tap, 1)
                    else:
                        act.activation(dst, src, ACT.Copy).then_inc(s_copied, 1)
                pairs(act, evacuate)

            @block.vector
            def _(dve):
                chain = Chain(dve, s_dve)
                dve.wait_ge(s_cact, 2)
                chain.link(dve.tensor_scalar(CACT[:, :], CACT[:, :], 1.0, 0.5, ALU.add, ALU.mult))
                chain.link(dve.tensor_tensor(CACT[:, :], CACT[:, :], PRM[:, PC["c"]:PC["c"] + KD], ALU.mult))
                prev = [0, 0]
                for k in range(KD):
                    dve.wait_ge(s_wada[k], 16)
                    for h in range(2):
                        a = ACC[:, h * D:(h + 1) * D]
                        w = WA[k][:, h * D:(h + 1) * D]
                        if k == 0:
                            prev[h] = chain.sig(dve.tensor_scalar(a, w, CACT[:, 0:1], None, ALU.mult))
                        else:
                            chain.upto(prev[h])
                            prev[h] = chain.sig(dve.scalar_tensor_tensor(out=a, in0=w, scalar=CACT[:, k:k + 1], in1=a,
                                                                         op0=ALU.mult, op1=ALU.add))
                chain.upto(prev[1])
                dve.sem_inc(s_acc, 1)
                dve.wait_ge(s_ss, TT)
                chain.link(dve.tensor_scalar(SS[:, :], SS[:, :], 1.0 / D, NORM_EPS, ALU.mult, ALU.add))
                dve.reciprocal(SS[:, :], SS[:, :]).then_inc(s_rs, 1)
                dve.wait_ge(s_mod, 1)
                chain.link(dve.tensor_tensor(AM[:, :], PS[:, 4, KD:2 * KD], PRM[:, PC["b_scale"]:PC["b_scale"] + KD], ALU.add))
                dve.scalar_tensor_tensor(out=AM[:, :], in0=AM[:, :], scalar=1.0, in1=PRM[:, PC["g_pre"]:PC["g_pre"] + KD],
                                         op0=ALU.add, op1=ALU.mult).then_inc(s_am, 1)
                dve.tensor_tensor(BM[:, :], PS[:, 4, 0:KD], PRM[:, PC["b_shift"]:PC["b_shift"] + KD], ALU.add).then_inc(s_am, 1)
                dve.wait_ge(s_am, 2)
                for j in range(1, 2 * KD, 2):
                    dve.wait_ge(s_tr, j + 1)
                    dve.tensor_scalar(HT[:, j // 2, HALF:2 * HALF], PS[:, j % 4], AM[:, j // 2:j // 2 + 1],
                                      BM[:, j // 2:j // 2 + 1], ALU.mult, ALU.add).then_inc(s_ht[1], 1)
                def taps(n, slot, u, conv, k, run):
                    if not conv:
                        return
                    dve.wait_ge(s_tap, n + 1)
                    src = PS[:, 4 + 2 * u:6 + 2 * u].rearrange("p a b -> p (a b)")
                    dst = PJ[:, ds(slot, 1), :].rearrange("p a b -> p (a b)")
                    left = PRM[:, ds(PC["taps"] + (slot - R0), 1)]
                    right = PRM[:, ds(PC["taps"] + 2 * NCONV + (slot - R0), 1)]
                    dve.scalar_tensor_tensor(out=dst[:, 1:T], in0=src[:, 0:T - 1], scalar=left, in1=dst[:, 1:T],
                                             op0=ALU.mult, op1=ALU.add).then_inc(s_dve, 1)
                    dve.wait_ge(s_dve, chain.n + n + 1)
                    dve.scalar_tensor_tensor(out=dst[:, 0:T - 1], in0=src[:, 1:T], scalar=right, in1=dst[:, 0:T - 1],
                                             op0=ALU.mult, op1=ALU.add).then_inc(s_shifted, 1)
                pairs(dve, taps, RUNS[:2])

            @block.tensor
            def _(pe):
                pe.sem_inc(s_mm, 2)
                pe.wait_ge(s_acc, 1)
                for j in range(2 * KD):
                    m = pe.matmul(PS[:, 4, j:j + 1], ACC[:, j * P:(j + 1) * P], ONES[:, 0:1], start=True, stop=True)
                m.then_inc(s_mod, 1)
                pe.wait_ge(s_xn, TT)
                for j in range(2 * KD):
                    if j >= 4:
                        pe.wait_ge(s_ht[j % 2], (j - 4) // 2 + 1)
                    for t in range(4):
                        m = pe.transpose(PS[:, j % 4, t * P:(t + 1) * P],
                                         X[:, (j % 2) * 4 + t, (j // 2) * P:(j // 2 + 1) * P], IDN[:, :])
                    m.then_inc(s_tr, 1)
                pe.wait_ge(s_ht[0], KD)
                pe.wait_ge(s_ht[1], KD)

                pe.sem_inc(s_shifted, 2)
                def project(n, slot, u, conv, k, run):
                    pe.wait_ge(s_w[u], 16 * (k + 1))
                    if run < 2 or (run == 2 and u == 0):
                        pe.wait_ge(s_shifted, n + 1)
                    else:
                        pe.wait_ge(s_copied, n - (NCONV + 1))
                    for half in range(2):
                        for kk in range(KD):
                            m = pe.matmul(PS[:, 4 + 2 * u + half], WR[:, u, kk, :], HT[:, kk, half * HALF:(half + 1) * HALF],
                                          start=(kk == 0), stop=(kk == KD - 1))
                    m.then_inc(s_mm, 1)
                pairs(pe, project)



def norm_and_rotate(nc, sem, PJ, HT, PRM, IDN, PS, prm, consts):
    with ExitStack() as st:
        sb = lambda name, shape, dt=F32: st.enter_context(nc.sbuf_tensor(name, shape, dt))
        KK = HT[:, 0:4, :]
        VT = HT[:, 4:8, :].rearrange("p a b -> p (a b)").rearrange("p (c n) -> p c n", c=TT)
        ROT = sb("ROT", [P, P])
        ROWS = sb("ROWS", [P, 9, 32])
        SPE = sb("SPE", [32, 9 * P + 1])
        SPR, EPS = SPE[:, 0:9 * P].rearrange("p (j m) -> p j m", m=P), SPE[:, 9 * P:9 * P + 1]
        CS = sb("CS", [P, 2, T])
        SQ = sb("SQ", [P, 4, T])
        QC = sb("QC", [P, 2, T])
        QS = sb("QS", [P, T])
        RST = sb("RST", [32, T])

        s_cst, s_wa, s_vt, s_vtc = sem("consts2_loaded"), sem("wd_tanh"), sem("v_transposed"), sem("v_copied")
        s_sq, s_sums, s_var, s_rst = sem("squares_ready"), sem("sums_of_squares"), sem("inverse_squares"), sem("inverse_norms")
        s_spr, s_unit, s_rot, s_cosd, s_roped = sem("norms_spread"), sem("normed"), sem("rotated"), sem("times_cos"), sem("roped")
        s_dve = sem("dve_chain2")
        slot = lambda j: PJ[:, j, :]
        source = lambda j: slot(RK0 + j) if j < 4 else slot(Q0 + j - 4)
        banks = lambda b: PS[:, b:b + 2].rearrange("p a b -> p (a b)")

        with nc.Block() as block:
            @block.sync
            def _(sp):
                for dst, name, w, rows in ((ROWS[:, :, :].rearrange("p a b -> p (a b)"), "rows", 9 * 32, P), (ROT[:, :], "rot", P, P),
                                           (SPE[:, :], "spread", 9 * P + 1, 32), (CS[:, 0], "cos", T, P), (CS[:, 1], "sin", T, P)):
                    sp.dma_start(dst, consts[0:rows, CC[name]:CC[name] + w]).then_inc(s_cst, 16)

            @block.gpsimd
            def _(pool):
                pool.wait_ge(s_cst, 80)
                for j in range(5):
                    pool.wait_ge(s_unit, 4 + j + 1)
                    if j >= 2:
                        pool.wait_ge(s_roped, j - 1)
                    pool.tensor_tensor(QC[:, j % 2], slot(Q0 + j), CS[:, 0], ALU.mult).then_inc(s_cosd, 1)

            @block.scalar
            def _(act):
                act.activation(PJ[0:RANK, WA0, :], PJ[0:RANK, WA0, :], ACT.Tanh).then_inc(s_wa, 1)
                for c in range(TT):
                    act.wait_ge(s_vt, c + 1)
                    act.activation(VT[:, c, :], PS[:, 6 + c % 2], ACT.Copy).then_inc(s_vtc, 1)
                for j in range(9):
                    if j >= 4:
                        act.wait_ge(s_sums, j - 3)
                    act.activation(SQ[:, j % 4], source(j), ACT.Square, scale=prm("k_k", j) if j < 4 else HD ** -0.5).then_inc(s_sq, 1)
                act.wait_ge(s_var, 1)
                act.activation(RST[:, :], RST[:, :], ACT.Sqrt).then_inc(s_rst, 1)

            @block.vector
            def _(dve):
                chain = Chain(dve, s_dve)
                dve.wait_ge(s_cst, 80)
                dve.wait_ge(s_sums, 9)
                chain.link(dve.tensor_scalar(RST[:, :], PS[0:32, 0:2].rearrange("p a b -> p (a b)"), EPS[:, 0:1], None, ALU.add))
                dve.reciprocal(RST[:, :], RST[:, :]).then_inc(s_var, 1)

                def rope(j):
                    dve.wait_ge(s_rot, j + 1)
                    chain.link(dve.tensor_tensor(QS[:, :], banks(6), CS[:, 1], ALU.mult))
                    dve.wait_ge(s_cosd, j + 1)
                    dve.tensor_tensor(slot(Q0 + j), QC[:, j % 2], QS[:, :], ALU.add).then_inc(s_roped, 1)

                for j in range(9):
                    dve.wait_ge(s_spr, j + 1)
                    g = prm("k_k", j) if j < 4 else prm("q_g") if j < 8 else prm("k_g")
                    dst = KK[:, j] if j < 4 else source(j)
                    dve.scalar_tensor_tensor(out=dst, in0=source(j), scalar=g, in1=banks(2 + 2 * (j % 2)),
                                             op0=ALU.mult, op1=ALU.mult).then_inc(s_unit, 1)
                    if j >= 5:
                        rope(j - 5)
                rope(4)

            @block.tensor
            def _(pe):
                for c in range(TT):
                    if c >= 2:
                        pe.wait_ge(s_vtc, c - 1)
                    for p in range(PAIRS):
                        m = pe.transpose(PS[:, 6 + c % 2, p * P:(p + 1) * P], PJ[:, RV0 + p, c * P:(c + 1) * P], IDN[:, :])
                    m.then_inc(s_vt, 1)
                pe.wait_ge(s_cst, 80)
                for j in range(9):
                    pe.wait_ge(s_sq, j + 1)
                    for half in range(2):
                        m = pe.matmul(PS[0:32, half], ROWS[:, j, :], SQ[:, j % 4, half * HALF:(half + 1) * HALF],
                                      start=(j == 0), stop=(j == 8))
                    m.then_inc(s_sums, 1)
                pe.wait_ge(s_rst, 1)
                pe.wait_ge(s_vtc, TT)

                def rotate(j):
                    pe.wait_ge(s_unit, 4 + j + 1)
                    if j >= 1:
                        pe.wait_ge(s_roped, j)
                    for half in range(2):
                        m = pe.matmul(PS[:, 6 + half], ROT[:, :], PJ[:, Q0 + j, half * HALF:(half + 1) * HALF], start=True, stop=True)
                    m.then_inc(s_rot, 1)

                for j in range(9):
                    if j >= 2:
                        pe.wait_ge(s_unit, j - 1)
                    for half in range(2):
                        m = pe.matmul(PS[:, 2 + 2 * (j % 2) + half], SPR[:, j, :], RST[:, half * HALF:(half + 1) * HALF], start=True, stop=True)
                    m.then_inc(s_spr, 1)
                    if j >= 5:
                        rotate(j - 5)
                rotate(4)


def prepare_units(nc, sem, PJ, HT, PRM, EMU, PS, prm, w_up, a_up, consts, units):
    with ExitStack() as st:
        sb = lambda name, shape, dt=F32: st.enter_context(nc.sbuf_tensor(name, shape, dt))
        KK = HT[:, 0:4, :]
        VT = HT[:, 4:8, :].rearrange("p a b -> p (a b)").rearrange("p (c n) -> p c n", c=TT)
        BLK = sb("BLK", [P, P])
        START = sb("START", [P, T])
        UP = sb("UP", [P, 2, 2, P])
        KAC = sb("KAC", [P, PAIRS])
        TW = sb("TW", [P, 2, T])
        TA = sb("TA", [P, 2, T])
        FF = sb("FF", [P, 2, T])
        MU = sb("MU", [P, 2, TT])
        OB = sb("OB", [P, 2, 4, T])

        s_cst, s_zero, s_up, s_pre = sem("consts3_loaded"), sem("up_zeroed"), [sem("up_loaded0"), sem("up_loaded1")], sem("pre_activations_plus_2")
        s_tw, s_ta, s_g, s_e = sem("tanh_w"), sem("tanh_a_plus_1"), sem("exponents_ready"), [sem(f"exp{k}_ready") for k in range(3)]
        s_u, s_kt, s_kq, s_rr, s_ai, s_ki = (sem(n) for n in ("u_ready", "kt_ready", "kq_ready", "rr_ready", "ai_ready_plus_2", "ki_ready"))
        s_st = [sem(f"stored{z}_plus_16") for z in range(2)]
        s_vst = sem("v_stored")
        s_prod, s_bsum, s_bon, s_dve, s_hp, s_mu = sem("bonus_product"), sem("bonus_summed"), sem("bonus_ready"), sem("dve_chain3"), sem("halves_ready"), sem("emu_ready")
        dyn = lambda a, j: a[:, ds(j, 1), :].rearrange("p a b -> p (a b)")
        banks = lambda b: PS[:, b:b + 2].rearrange("p a b -> p (a b)")
        chunks = lambda a: a.rearrange("p (c n) -> p c n", c=TT)

        with nc.Block() as block:
            @block.sync
            def _(sp):
                sp.dma_start(BLK[:, :], consts[:, CC["blocks"]:CC["blocks"] + P]).then_inc(s_cst, 16)
                sp.dma_start(START[:, :], consts[:, CC["start"]:CC["start"] + T]).then_inc(s_cst, 16)
                for z in range(2):
                    for p in range(PAIRS):
                        sp.dma_start(units[z, p * TT:(p + 1) * TT, :, 4, :].rearrange("c p n -> p c n"),
                                     VT[:, ORDER[z], p * P:(p + 1) * P]).then_inc(s_vst, 16)
                sp.wait_ge(s_zero, 1)
                for z in range(2):
                    sp.sem_inc(s_st[z], 16)
                with sp.Fori(0, PAIRS) as p:
                    for z in range(2):
                        sp.wait_ge(s_pre, 2 * p + z + 1)
                        sp.dma_start(UP[0:RANK, z, 0, :], w_up[z, :, ds(p * P, P)]).then_inc(s_up[z], 16)
                        sp.dma_start(UP[RANK:P, z, 1, :], a_up[z, :, ds(p * P, P)]).then_inc(s_up[z], 16)
                sp.wait_ge(s_vst, 16 * 2 * PAIRS)

            @block.gpsimd
            def _(pool):
                pool.memset(UP[:, :, :, :], 0.0).then_inc(s_zero, 1)
                for n in range(2 * PAIRS):
                    p, z = n // 2, n % 2
                    pool.wait_ge(s_u, n + 1)
                    pool.tensor_tensor(OB[:, z, 3], OB[:, z, 3], PJ[:, RK0 + p, :], ALU.mult).then_inc(s_kt, 1)
                    pool.wait_ge(s_e[0], n + 1)
                    pool.tensor_tensor(OB[:, z, 0], OB[:, z, 0], KK[:, p], ALU.mult).then_inc(s_kq, 1)

            @block.scalar
            def _(act):
                act.sem_inc(s_ta, 1)
                act.wait_ge(s_hp, 1)
                with act.Fori(0, PAIRS) as p:
                    for z in range(2):
                        n = 2 * p + z + 1
                        act.wait_ge(s_pre, n + 2)
                        act.activation(TW[:, z], banks(0), ACT.Tanh, scale=0.5, bias=PRM[:, ds(PC["w0"] + PAIRS * z + p, 1)]).then_inc(s_tw, 1)
                        act.wait_ge(s_ai, n)
                        act.activation(TA[:, z], banks(2), ACT.Tanh, scale=0.5, bias=PRM[:, ds(PC["a0"] + PAIRS * z + p, 1)]).then_inc(s_ta, 1)
                    for z in range(2):
                        n = 2 * p + z + 1
                        act.wait_ge(s_g, n)
                        act.wait_ge(s_st[z], 64 * p + 16)
                        incl, excl = (FF, TW) if z == 0 else (TW, FF)
                        act.activation(OB[:, z, 0], excl[:, z], ACT.Exp).then_inc(s_e[0], 1)
                        act.activation(OB[:, z, 2], incl[:, z], ACT.Exp, scale=-1.0).then_inc(s_e[2], 1)
                        act.activation(OB[:, z, 1], incl[:, z], ACT.Exp).then_inc(s_e[1], 1)
                        act.activation(EMU[:, ds((PAIRS * z + p) * TT, TT)], MU[:, z, ORDER[z]], ACT.Exp).then_inc(s_mu, 1)
                    for z in range(2):
                        n = 2 * p + z + 1
                        for a, s_a, more in ((0, s_kq, 0), (3, s_ki, 0), (2, s_ai, 2), (1, s_rr, 0)):
                            act.wait_ge(s_a, n + more)
                            act.dma_start(units[z, ds(p * TT, TT), :, a, :].rearrange("c p n -> p c n"),
                                          chunks(OB[:, z, a])[:, ORDER[z], :]).then_inc(s_st[z], 16)
                for z in range(2):
                    act.wait_ge(s_st[z], 64 * PAIRS + 16)

            @block.vector
            def _(dve):
                chain = Chain(dve, s_dve)
                w = PC["a0"] + 2 * PAIRS
                halves = PRM[:, PC["w0"]:w]
                dve.tensor_scalar(halves, halves, 0.5, None, ALU.mult).then_inc(s_dve, 1)
                ka = PRM[:, PC["k_a"]:PC["k_a"] + PAIRS]
                dve.tensor_scalar(ka, ka, 0.5, None, ALU.mult).then_inc(s_dve, 1)
                dve.wait_ge(s_dve, 2)
                dve.tensor_scalar(KAC[:, :], ka, -1.0, 1.0, ALU.mult, ALU.add).then_inc(s_hp, 1)
                dve.wait_ge(s_hp, 1)
                dve.wait_ge(s_cst, 32)
                dve.sem_inc(s_ai, 2)
                chain.base = 2
                with dve.Fori(0, PAIRS) as p:
                    PER = 8 + 2
                    chain.base, chain.n = 2 + PER * p, 0
                    for z in range(2):
                        n = 2 * p + z + 1
                        dve.wait_ge(s_tw, n)
                        chain.link(dve.tensor_scalar(TW[:, z], TW[:, z], 1.0, -0.5 * DECAY, ALU.add, ALU.mult))
                        chain.link(dve.tensor_tensor_scan(FF[:, z], START[:, :], TW[:, z], 0.0, ALU.mult, ALU.add))
                        if z == 0:
                            dve.wait_ge(s_tw, n)
                        chain.link(dve.tensor_scalar(MU[:, z, :], chunks(FF[:, z])[:, :, P - 1], 0.5, None, ALU.mult))
                        mu = MU[:, z, :].unsqueeze(2).broadcast_to((P, TT, P))
                        a, b = (chunks(FF[:, z]), mu) if z == 0 else (mu, chunks(FF[:, z]))
                        chain.link(dve.tensor_tensor(chunks(FF[:, z]), a, b, ALU.subtract))
                        dve.tensor_tensor(TW[:, z], FF[:, z], TW[:, z], ALU.subtract if z == 0 else ALU.add).then_inc(s_g, 1)
                        dve.wait_ge(s_ta, n + 1)
                        dve.wait_ge(s_st[z], 64 * p + 16)
                        dve.tensor_scalar(OB[:, z, 3], TA[:, z], PRM[:, ds(PC["k_a"] + p, 1)], KAC[:, ds(p, 1)],
                                          ALU.mult, ALU.add).then_inc(s_u, 1)
                        chain.sig(dve.scalar_tensor_tensor(out=TA[:, z], in0=TA[:, z], scalar=1.0, in1=dyn(KK, p),
                                                           op0=ALU.add, op1=ALU.mult))
                    for z in range(2):
                        n = 2 * p + z + 1
                        dve.wait_ge(s_kt, n)
                        dve.wait_ge(s_e[1], n)
                        dve.scalar_tensor_tensor(out=FF[:, z], in0=dyn(PJ, R0 + p), scalar=PRM[:, ds(PC["r_k"] + p, 1)],
                                                 in1=OB[:, z, 3], op0=ALU.mult, op1=ALU.mult).then_inc(s_prod, 1)
                        dve.wait_ge(s_prod, n)
                        dve.tensor_tensor(OB[:, z, 3], OB[:, z, 3], OB[:, z, 2], ALU.mult).then_inc(s_ki, 1)
                        chain.upto(5 * (z + 1))
                        dve.wait_ge(s_ki, n)
                        dve.scalar_tensor_tensor(out=OB[:, z, 2], in0=TA[:, z], scalar=-0.5, in1=OB[:, z, 2],
                                                 op0=ALU.mult, op1=ALU.mult).then_inc(s_ai, 1)
                        dve.tensor_tensor(OB[:, z, 1], OB[:, z, 1], dyn(PJ, R0 + p), ALU.mult).then_inc(s_rr, 1)
                    dve.wait_ge(s_bsum, p + 1)
                    dve.tensor_tensor(dyn(PJ, RV0 + p), banks(4), dyn(PJ, RV0 + p), ALU.mult).then_inc(s_bon, 1)
                    assert chain.n == PER

            @block.tensor
            def _(pe):
                pe.sem_inc(s_pre, 2)
                pe.wait_ge(s_cst, 32)

                def pre(p):
                    for z in range(2):
                        pe.wait_ge(s_up[z], 32 * (p + 1))
                        pe.wait_ge(s_ta, 2 * p + z + 1)
                        for k in range(2):
                            for half in range(2):
                                m = pe.matmul(PS[:, 2 * k + half], UP[:, z, k, :], PJ[:, WA0, half * HALF:(half + 1) * HALF],
                                              start=True, stop=True)
                        m.then_inc(s_pre, 1)

                def bonus(p, first=False):
                    for z in range(2):
                        pe.wait_ge(s_prod, 2 * p + z + 1)
                        if z == 0 and not first:
                            pe.wait_ge(s_bon, p)
                        for half in range(2):
                            m = pe.matmul(PS[:, 4 + half], BLK[:, :], FF[:, z, half * HALF:(half + 1) * HALF],
                                          start=(z == 0), stop=(z == 1))
                    m.then_inc(s_bsum, 1)
                pre(0)
                pre(1)
                bonus(0, True)
                with pe.Fori(1, PAIRS - 1) as p:
                    pre(p + 1)
                    bonus(p)
                bonus(PAIRS - 1)


def key_products(nc, sem, PJ, PS, units):
    with ExitStack() as st:
        sb = lambda name, shape, dt=F32: st.enter_context(nc.sbuf_tensor(name, shape, dt))
        KX = sb("KX1", [P, 4, 2, P])
        AI = sb("AI1", [P, 4, P])
        ND, NT = block_views(PJ)
        s_zero, s_ld = sem("kx_zeroed"), [sem(f"products_loaded{r}") for r in range(4)]
        s_g, s_act, s_dve, s_nt = sem("product_done_plus_4"), sem("blocks_by_act_plus_2"), sem("blocks_by_dve_plus_2"), sem("blocks_turned")
        with nc.Block() as block:
            @block.gpsimd
            def _(pool):
                pool.memset(KX[:, :, :, :], 0.0).then_inc(s_zero, 1)

            @block.sync
            def _(sp):
                sp.wait_ge(s_zero, 1)
                with sp.Fori(0, STEPS // 2) as i:
                    for r in range(4):
                        z, m = r % 2, 2 * i + r // 2
                        sp.wait_ge(s_g, 4 * i + r + 1)
                        for h in range(2):
                            rows = slice(h * HD, (h + 1) * HD)
                            sp.dma_start(KX[rows, r, h, :], units[z, ds(m, 1), rows, 0, :].rearrange("o p n -> p (o n)")).then_inc(s_ld[r], 16)
                        sp.dma_start(AI[:, r, :], units[z, ds(m, 1), :, 2, :].rearrange("o p n -> p (o n)")).then_inc(s_ld[r], 16)

            @block.tensor
            def _(pe):
                pe.sem_inc(s_g, 4)
                with pe.Fori(0, STEPS // 2) as i:
                    for r in range(4):
                        n = 4 * i + r + 1
                        pe.wait_ge(s_ld[r], 48 * (i + 1))
                        pe.wait_ge(s_act, n)
                        pe.wait_ge(s_dve, n)
                        pe.matmul(PS[:, r % 2, 0:2 * P], AI[:, r, :], KX[:, r].rearrange("p h n -> p (h n)"),
                                  start=True, stop=True).then_inc(s_g, 1)

            def take(eng, copy, quads, s_mine, other):
                eng.sem_inc(s_mine, 2)
                with eng.Fori(0, STEPS // 2) as i:
                    for r in range(4):
                        z, n = r % 2, 4 * i + r + 1
                        eng.wait_ge(s_g, n + 4)
                        if other is not None:
                            eng.wait_ge(other, n + 2)
                        for q in quads:
                            rows = slice(32 * q, 32 * q + 32)
                            last = copy(ND[z][rows, ds(2 * (2 * i + r // 2), 2), :],
                                        PS[rows, r % 2, 0:2 * P].rearrange("p (h n) -> p h n", h=2)[:, :, 32 * q:32 * q + 32])
                        last.then_inc(s_mine, 1)

            @block.scalar
            def _(act):
                take(act, lambda o, i: act.activation(o, i, ACT.Copy), (0, 1), s_act, None)

            @block.vector
            def _(dve):
                take(dve, lambda o, i: dve.tensor_copy(o, i), (2, 3), s_dve, None)
                dve.wait_ge(s_act, 2 * STEPS + 2)
                dve.wait_ge(s_dve, 2 * STEPS + 2)
                for z in range(2):
                    for half in range(2):
                        src = ND[z][:, 32 * half:32 * half + 32, :].rearrange("p g t -> p t g")
                        dst = NT[:, 2 * z + half].rearrange("p (a b) -> p a b", a=32)
                        dve.transpose(dst if z == 0 else dst.rearrange("p a b -> p b a"), src).then_inc(s_nt, 1)
                dve.wait_ge(s_nt, 4)


def block_views(PJ):
    flat = lambda j: PJ[:, j:j + 4, :].rearrange("p a b -> p (a b)")
    nd = flat(R0).rearrange("p (z g t) -> p z g t", z=2, t=32)
    return [nd[:, 0], nd[:, 1]], PJ[:, RK0:RK0 + 4, :]


def attend(nc, sem, PJ, PRM, IDN, PS, INV):
    with ExitStack() as st:
        sb = lambda name, shape, dt=F32: st.enter_context(nc.sbuf_tensor(name, shape, dt))
        KHL = sb("KHL", [P, KVH, T], F32R)
        QH, QL = sb("QH", [P, 2, T], F32R), sb("QL", [P, 2, T], F32R)
        VA = sb("VA", [P, KVH, TT, P])
        ONE = sb("ONE", [P, P], F32R)
        PB = sb("PB", [P, 2, HALF])
        MX = sb("MX", [P, 2])
        DG = sb("DGM", [P, 2, HALF], F32R)
        TG = sb("TG", [P, T])
        RD = sb("RD", [HD, HALF])
        NX = sb("NX", [P, HALF])
        TMP = sb("TMP", [P, 4, 16 * 17])

        _, NT = block_views(PJ)
        XS = PJ[:, R0:R0 + 4, :].rearrange("p b (i c) -> p b i c", c=32)
        s_vtr, a_va, a_va2, d_one = sem("va_transposed"), sem("va_ready_plus_2"), sem("two_ready"), sem("one_ready")
        a_kh, d_kl = sem("k_hi_ready"), sem("k_lo_ready")
        a_qh, d_ql = sem("q_hi_ready"), sem("q_lo_ready")
        s_s, d_mx, d_dg = sem("scores_ready"), sem("max_ready_plus_2"), sem("minus_max_ready")
        s_st, a_p, s_pv, d_o = sem("scores_t_ready_plus_32"), sem("weights_ready_plus_2"), sem("outputs_summed_plus_2"), sem("output_taken_plus_2")
        a_tg, d_gate, d_rd, d_nx = sem("gate_tanh"), sem("gate_ready_plus_1"), sem("rden_ready"), sem("normalised")
        g_sub, d_inv = sem("pool_chain"), sem("inverses_turned")
        banks = lambda b: PS[:, b:b + 2].rearrange("p a b -> p (a b)")
        dyn = lambda j, rows=slice(0, P): PJ[rows, ds(j, 1), :].rearrange("p a b -> p (a b)")
        half_rows = lambda h: slice(h * HD, (h + 1) * HD)

        with nc.Block() as block:
            @block.gpsimd
            def _(pool):
                pool.memset(VA[:, :, :, HD:P], 2.0).then_inc(a_va2, 1)
                chain = Chain(pool, g_sub)
                chain.link(pool.memset(XS, 0.0))
                chain.link(pool.memset(PJ[:, R0:R0 + 4, 0:T:33], 1.0))
                nt = NT.rearrange("p b (i j) -> p b i j", j=32)
                for j in range(31):
                    low, left = 31 - j, j + 1
                    t = TMP[:, :, 0:low * left].rearrange("p b (i c) -> p b i c", c=left)
                    n_col = nt[:, :, j + 1:32, j].unsqueeze(3).broadcast_to((P, 4, low, left))
                    x_row = XS[:, :, j, 0:left].unsqueeze(2).broadcast_to((P, 4, low, left))
                    chain.link(pool.tensor_tensor(t, n_col, x_row, ALU.mult))
                    dst = XS[:, :, j + 1:32, 0:left]
                    chain.link(pool.tensor_tensor(dst, dst, t, ALU.add))

            @block.scalar
            def _(act):
                for kv in range(KVH):
                    act.activation(KHL[half_rows(kv), kv], PJ[half_rows(kv), K0, :], ACT.Copy).then_inc(a_kh, 1)
                act.sem_inc(a_va, 2)
                for c in range(TT):
                    act.wait_ge(s_vtr, c + 1)
                    act.activation(VA[:, :, c, 0:HD], PS[:, 4 + c % 2, 0:P].rearrange("p (a b) -> p a b", a=2), ACT.Copy).then_inc(a_va, 1)
                act.sem_inc(a_p, 2)
                with act.Fori(0, PAIRS) as p:
                    for h in range(2):
                        act.wait_ge(s_st, 16 * (2 * p + h + 1))
                        for part in range(2):
                            last = act.activation(QH[half_rows(part), h], dyn(Q0 + p, half_rows(h)), ACT.Copy)
                        last.then_inc(a_qh, 1)
                    act.wait_ge(d_gate, p + 1)
                    act.activation(TG[:, :], dyn(GA0 + p), ACT.Tanh, scale=0.5).then_inc(a_tg, 1)
                    for u in range(4):
                        for k in range(TT):
                            g = 8 * (4 * p + u) + k
                            act.wait_ge(s_st, g + 33)
                            act.wait_ge(s_pv, g + 1)
                            act.activation(PB[:, k % 2], PS[:, 4 + k % 2], ACT.Exp, scale=HD ** -0.5).then_inc(a_p, 1)

            @block.vector
            def _(dve):
                dve.tensor_scalar(ONE[:, :], IDN[:, :], 0.0, 1.0, ALU.mult, ALU.add).then_inc(d_one, 1)
                for kv in range(KVH):
                    r = half_rows(kv)
                    dve.wait_ge(a_kh, kv + 1)
                    dve.tensor_tensor(KHL[half_rows(1 - kv), kv], PJ[r, K0, :], KHL[r, kv].bitcast(F32), ALU.subtract).then_inc(d_kl, 1)
                dve.sem_inc(d_mx, 2)
                dve.sem_inc(d_o, 2)
                dve.sem_inc(d_gate, 1)
                dve.wait_ge(d_one, 1)

                def lows(p, h):
                    dve.wait_ge(a_qh, 2 * p + h + 1)
                    for part in range(2):
                        last = dve.tensor_tensor(QL[half_rows(part), h], dyn(Q0 + p, half_rows(h)), QH[half_rows(h), h].bitcast(F32), ALU.subtract)
                    last.then_inc(d_ql, 1)

                def maxima(p, u):
                    dve.wait_ge(s_st, 8 * (4 * p + u) + 24)
                    for t in range(4):
                        c = 4 * (4 * p + u) + t
                        dve.wait_ge(s_s, c + 1)
                        dve.reduce_max(MX[:, t % 2:t % 2 + 1], banks(2 * (t % 2)), AXX).then_inc(d_mx, 1)
                        dve.wait_ge(d_mx, c + 3)
                        dve.tensor_scalar(DG[:, u % 2, t * P:(t + 1) * P], IDN[:, :], MX[:, t % 2:t % 2 + 1], -1.0,
                                          ALU.mult, ALU.mult).then_inc(d_dg, 1)

                def finish(p, u):
                    n, r, cols = 4 * p + u, half_rows(u // 2), slice((u % 2) * HALF, (u % 2 + 1) * HALF)
                    dve.wait_ge(s_pv, 8 * n + 10)
                    dve.reciprocal(RD[:, :], PS[HD:P, 6 + u % 2]).then_inc(d_rd, 1)
                    dve.wait_ge(d_rd, n + 1)
                    dve.tensor_tensor(NX[r, :], PS[0:HD, 6 + u % 2], RD[:, :], ALU.mult).then_inc(d_o, 1)
                    dve.wait_ge(d_o, n + 3)
                    o = dyn(GA0 + p, r)[:, cols]
                    dve.tensor_tensor(o, o, NX[r, :], ALU.mult).then_inc(d_nx, 1)
                with dve.Fori(0, PAIRS) as p:
                    lows(p, 0)
                    maxima(p, 0)
                    lows(p, 1)
                    dve.wait_ge(a_tg, p + 1)
                    dve.scalar_tensor_tensor(out=dyn(GA0 + p), in0=TG[:, :], scalar=1.0, in1=dyn(GA0 + p),
                                             op0=ALU.add, op1=ALU.mult).then_inc(d_gate, 1)
                    for u in range(4):
                        if u < 3:
                            maxima(p, u + 1)
                        if u == 0:
                            dve.wait_ge(d_gate, p + 2)
                        finish(p, u)
                dve.wait_ge(g_sub, 2 + 2 * 31)
                for z in range(2):
                    for half in range(2):
                        x = XS[:, 2 * z + half]
                        by_row, by_col = x.rearrange("p i c -> p c i"), x
                        if z == 1:
                            by_row, by_col = by_col, by_row
                        for k, src in ((0, by_row), (1, by_col)):
                            dst = INV[k][z][:, 32 * half:32 * half + 32, :].rearrange("p g n -> p n g")
                            dve.transpose(dst, src).then_inc(d_inv, 1)
                dve.wait_ge(d_inv, 8)

            @block.tensor
            def _(pe):
                pe.sem_inc(s_st, 32)
                pe.sem_inc(s_pv, 2)
                for c in range(TT):
                    if c >= 2:
                        pe.wait_ge(a_va, c + 1)
                    pe.transpose(PS[:, 4 + c % 2, 0:P], PJ[:, V0, c * P:(c + 1) * P], IDN[:, :]).then_inc(s_vtr, 1)
                pe.wait_ge(a_va, TT + 2)
                pe.wait_ge(a_va2, 1)
                pe.wait_ge(d_one, 1)
                pe.wait_ge(d_kl, KVH)

                def scores(kv, p, u, t, half):
                    if half == 0:
                        pe.wait_ge(d_mx, 4 * (4 * p + u) + t + 1)
                    q = slice((u % 2) * HALF + t * P, (u % 2) * HALF + (t + 1) * P)
                    for k, Q in enumerate((QH, QL)):
                        m = pe.matmul(PS[:, 2 * (t % 2) + half], Q[:, u // 2, q], KHL[:, kv, half * HALF:(half + 1) * HALF],
                                      start=(k == 0), stop=(k == 1))
                    if half == 1:
                        m.then_inc(s_s, 1)

                def scores_t(kv, p, u, k):
                    pe.wait_ge(a_p, 8 * (4 * p + u) + k + 1)
                    o, q, key = PS[:, 4 + k % 2], slice((u % 2) * HALF, (u % 2 + 1) * HALF), slice(k * P, (k + 1) * P)
                    pe.matmul(o, KHL[:, kv, key], QH[:, u // 2, q], start=True, stop=False)
                    pe.matmul(o, KHL[:, kv, key], QL[:, u // 2, q], start=False, stop=False)
                    pe.matmul(o, ONE[:, :], DG[:, u % 2, :], start=False, stop=True).then_inc(s_st, 1)

                def outputs(kv, p, u, k):
                    pe.wait_ge(a_p, 8 * (4 * p + u) + k + 3)
                    if k == 0:
                        pe.wait_ge(d_o, 4 * p + u + 1)
                    pe.matmul(PS[:, 6 + u % 2], VA[:, kv, k, :], PB[:, k % 2], start=(k == 0), stop=(k == TT - 1)).then_inc(s_pv, 1)

                for kv in range(KVH):
                    with pe.Fori(kv * (PAIRS // KVH), (kv + 1) * (PAIRS // KVH)) as p:
                        pe.wait_ge(d_ql, 2 * p + 1)
                        for t in range(4):
                            for half in range(2):
                                scores(kv, p, 0, t, half)
                        for u in range(4):
                            pe.wait_ge(d_dg, 4 * (4 * p + u) + 4)
                            if u == 1:
                                pe.wait_ge(d_ql, 2 * p + 2)
                            for k in range(TT):
                                scores_t(kv, p, u, k)
                                if u < 3:
                                    scores(kv, p, u + 1, k // 2, k % 2)
                                if k:
                                    outputs(kv, p, u, k - 1)
                            outputs(kv, p, u, TT - 1)


def state_passes(nc, sem, PJ, HT, IDN, EMU, CACT, PS, consts, units, INV, WO, GACC, w_out, w_ada):
    with ExitStack() as st:
        sb = lambda name, shape, dt=F32: st.enter_context(nc.sbuf_tensor(name, shape, dt))
        Y = [HT[:, 4 * z:4 * z + 4, :].rearrange("p a b -> p (a b)").rearrange("p (m n) -> p m n", n=P) for z in range(2)]
        KX = sb("KX", [P, 4, 2, 2, P])
        AK = sb("AK", [P, 4, 2, P])
        VZ = sb("VZ", [P, 4, 2 * P])
        MSK = sb("MSK", [P, 2, 4, P])
        BD = sb("BD", [P, 4, 32])
        DG = sb("DG", [P, 2, P])
        EM2 = sb("EM2", [P, 2 * STEPS])
        SA, SB = sb("SA", [P, 2, 2, 2, P]), sb("SB", [P, 2, 2, 2, P])
        TOK, RH, ZT = sb("TOK", [P, 2, 2 * P]), sb("RH", [P, 2, 2 * P]), sb("ZT", [P, 2, 2 * P])
        W, WU = sb("W", [P, 2, 2 * P]), sb("WU", [P, 2, 2 * P])
        WT = sb("WT", [P, 2, P])
        RE, ATB, HB = sb("RE", [P, 2, P]), sb("ATB", [P, 2, P]), sb("HB", [P, 2, P])
        PX, PT = sb("PX", [P, 2, 2, P]), sb("PT", [P, 2, 2, P])
        WG = sb("WG", [P, 2, D])
        KEEP = sb("KEEP", [P, STEPS])

        s_wg, g_acc, s_wo = [sem(f"w_gate_loaded{u}") for u in range(2)], sem("gate_sums"), sem("w_out_loaded")
        s_cst, s_zero, s_ld = sem("consts5_loaded"), sem("s3_zeroed"), [sem(f"unit_loaded{r}") for r in range(4)]
        d_px, s_dg = sem("inverses_expanded"), sem("diag_ready")
        s_g1, s_g2, s_mv, s_zt, s_w, s_wu, s_rey, s_at, s_h = (sem(n) for n in (
            "pe_g1", "pe_g2", "pe_mv", "pe_zt", "pe_w", "pe_wu_plus_2", "pe_rey", "pe_at_b_plus_4", "pe_h_plus_1"))
        d_sa, d_sb, d_w, d_re, d_at, d_y, d_em = (sem(n) for n in ("sa_ready_plus_1", "sb_ready_plus_1", "w_ready", "re_ready_plus_4", "at_ready", "y_added_plus_1", "em2_ready"))
        a_tok, a_rh, a_zt, a_wu, a_y, a_h = (sem(n) for n in ("tok_ready", "rh_ready_plus_1", "zt_ready", "wu_ready", "y0_ready_plus_1", "h_ready_plus_1"))

        with nc.Block() as block:
            @block.sync
            def _(sp):
                sp.dma_start(MSK[:, :, :, :].rearrange("p z k n -> p (z k n)"), consts[:, CC["mask"]:CC["mask"] + 8 * P]).then_inc(s_cst, 16)
                sp.dma_start(BD[:, :, :].rearrange("p a b -> p (a b)"), consts[:, CC["bd"]:CC["bd"] + P]).then_inc(s_cst, 16)
                sp.dma_start(KEEP[:, :], consts[:, CC["keep"]:CC["keep"] + STEPS]).then_inc(s_cst, 16)
                sp.wait_ge(s_zero, 1)
                with sp.Fori(0, STEPS // 2) as i:
                    for r in range(4):
                        z, m, n = r % 2, 2 * i + r // 2, 4 * i + r + 1
                        sp.wait_ge(d_re, n)
                        sp.wait_ge(s_at, n)
                        for h in range(2):
                            rows = slice(h * HD, (h + 1) * HD)
                            sp.dma_start(KX[rows, r, h], units[z, ds(m, 1), rows, 0:2, :].rearrange("o p a n -> p (o a) n")).then_inc(s_ld[r], 16)
                        sp.dma_start(AK[:, r], units[z, ds(m, 1), :, 2:4, :].rearrange("o p a n -> p (o a) n")).then_inc(s_ld[r], 16)
                        sp.dma_start(VZ[:, r, HD:HD + P], units[z, ds(m, 1), :, 4, :].rearrange("o p n -> p (o n)")).then_inc(s_ld[r], 16)
                for k in range(KD):
                    sp.dma_start(WO[k], w_out[k * P:(k + 1) * P, :]).then_inc(s_wo, 16)
                sp.wait_ge(s_wo, 16 * KD)

            @block.gpsimd
            def _(pool):
                for u in range(2):
                    pool.dma_start(WG[:, u], w_ada[u * P:(u + 1) * P, 2 * D:3 * D]).then_inc(s_wg[u], 16)
                pool.memset(KX[:, :, :, :, :], 0.0)
                pool.memset(ATB[:, :, :], 0.0)
                pool.memset(HB[:, :, :], 0.0)
                pool.memset(VZ[:, :, :], 0.0)
                pool.drain().then_inc(s_zero, 1)
                for k in range(KD):
                    pool.wait_ge(s_wg[k % 2], 16 * (k // 2 + 1))
                    dst = WG[:, k % 2] if k else GACC[:, :]
                    pool.tensor_scalar(dst, WG[:, k % 2], CACT[:, k:k + 1], None, ALU.mult).then_inc(g_acc, 1)
                    pool.wait_ge(g_acc, max(2 * k, 1))
                    if k:
                        pool.tensor_tensor(GACC[:, :], GACC[:, :], WG[:, k % 2], ALU.add).then_inc(g_acc, 1)
                        pool.wait_ge(g_acc, 2 * k + 1)
                    if k + 2 < KD:
                        pool.dma_start(WG[:, k % 2], w_ada[(k + 2) * P:(k + 3) * P, 2 * D:3 * D]).then_inc(s_wg[k % 2], 16)

            @block.tensor
            def _(pe):
                pe.sem_inc(s_wu, 2)
                pe.sem_inc(s_at, 4)
                pe.sem_inc(s_h, 1)
                pe.wait_ge(s_zero, 1)
                pe.wait_ge(s_cst, 48)

                def g1(n, r, i):
                    pe.wait_ge(s_ld[r], 64 * (i + 1))
                    pe.wait_ge(d_sa, n + 1)
                    pe.matmul(PS[:, 0], AK[:, r, 0], KX[:, r].rearrange("p h a n -> p (h a n)"), start=True, stop=True).then_inc(s_g1, 1)

                def g2(n, r):
                    pe.wait_ge(d_sb, n + 1)
                    pe.matmul(PS[:, 1], AK[:, r, 1], KX[:, r].rearrange("p h a n -> p (h a n)"), start=True, stop=True).then_inc(s_g2, 1)

                def tokens(n, r):
                    z = r % 2
                    pe.wait_ge(s_dg, n + 1)
                    pe.wait_ge(a_rh, n + 1)
                    for k in range(2):
                        pe.matmul(PS[:, 2, 2 * P + k * P:3 * P + k * P], AK[:, r, k], DG[:, z, :], start=True, stop=True)
                    pe.matmul(PS[:, 2, 0:HD], KX[:, r, 0, 0], DG[:, z, 0:HD], start=True, stop=True)
                    pe.matmul(PS[:, 2, 3 * HD:4 * HD], KX[:, r, 1, 0], DG[:, z, HD:P], start=True, stop=True)

                def values(n, r):
                    z = r % 2
                    pe.wait_ge(d_sb, n + 2)
                    for h in range(2):
                        m = pe.matmul(PS[:, 2, (1 + h) * HD:(2 + h) * HD], SB[:, z, h, 0], VZ[:, r, (1 + h) * HD:(2 + h) * HD], start=True, stop=True)
                    m.then_inc(s_mv, 1)
                    pe.wait_ge(d_sa, n + 2)
                    pe.wait_ge(d_px, n + 1)
                    if not (isinstance(n, int) and n == 0):
                        pe.wait_ge(d_w, 3 * n - 1)
                    for h in range(2):
                        m = pe.matmul(PS[:, 3, h * P:(h + 1) * P], PX[:, z, h], SA[:, z, h, 0], start=True, stop=True)
                    m.then_inc(s_zt, 1)

                def round_(n, r, k):
                    z = r % 2
                    if k == 0:
                        pe.wait_ge(a_zt, n + 1)
                        pe.wait_ge(a_rh, n + 2)
                        src = RH[:, z]
                    else:
                        pe.wait_ge(d_w, 3 * n + k)
                        src = W[:, (k - 1) % 2]
                    for h in range(2):
                        m = pe.matmul(PS[:, 4 - k % 2, h * P:(h + 1) * P], ZT[:, z, h * P:(h + 1) * P], src[:, h * P:(h + 1) * P], start=True, stop=True)
                    m.then_inc(s_w, 1)

                def solve(n, r):
                    z = r % 2
                    pe.wait_ge(d_w, 3 * n + 3)
                    pe.wait_ge(d_y, n + 1)
                    for h in range(2):
                        m = pe.matmul(PS[:, 5, h * P:(h + 1) * P], PT[:, z, h], W[:, 0, h * P:(h + 1) * P], start=True, stop=True)
                    m.then_inc(s_wu, 1)

                def outputs(n, r):
                    z = r % 2
                    pe.wait_ge(a_wu, n + 1)
                    pe.wait_ge(d_re, n + 4)
                    pe.wait_ge(a_y, n + 1)
                    for h in range(2):
                        o = PS[:, 6, h * P:(h + 1) * P]
                        pe.matmul(o, WU[:, z, h * P:(h + 1) * P], SA[:, z, h, 1], start=True, stop=False)
                        m = pe.matmul(o, VZ[:, r, h * P:(h + 1) * P], SB[:, z, h, 1], start=False, stop=True)
                    m.then_inc(s_rey, 1)
                    pe.wait_ge(a_h, n + 1)
                    pe.matmul(PS[:, 7, 0:P], WT[:, z], TOK[:, z, 0:P], start=True, stop=True)
                    pe.matmul(PS[:, 7, P:2 * P], TOK[:, z, 0:P], WU[:, z, HD:HD + P], start=True, stop=False)
                    pe.matmul(PS[:, 7, P:2 * P], TOK[:, z, P:2 * P], VZ[:, r, HD:HD + P], start=False, stop=False).then_inc(s_at, 1)

                def state(n, r):
                    z = r % 2
                    pe.wait_ge(d_re, n + 5)
                    pe.wait_ge(a_wu, n + 1)
                    if not (isinstance(n, int) and n == 0):
                        pe.wait_ge(a_h, n)
                    pe.matmul(PS[:, 5, 0:P], HB[:, z], RE[:, z], start=True, stop=True)
                    pe.wait_ge(d_at, n + 1)
                    pe.matmul(PS[:, 7, P:2 * P], ATB[:, z], HB[:, z], start=False, stop=True).then_inc(s_h, 1)

                def early(n, r, i):
                    return [lambda: g1(n, r, i), lambda: g2(n, r), lambda: tokens(n, r), lambda: values(n, r)]

                def tile(n, r, nxt, prev):
                    round_(n, r, 0)
                    if nxt: nxt[0]()
                    round_(n, r, 1)
                    if nxt: nxt[1]()
                    if prev: state(*prev)
                    round_(n, r, 2)
                    if nxt: nxt[2]()
                    solve(n, r)
                    if nxt: nxt[3]()
                    outputs(n, r)

                for part in early(0, 0, 0):
                    part()
                LASTI = STEPS // 2 - 1
                tile(0, 0, early(1, 1, 0), None)
                for r in (1, 2):
                    tile(r, r, early(r + 1, r + 1, 0), (r - 1, r - 1))
                tile(3, 3, early(4, 0, 1), (2, 2))
                with pe.Fori(1, LASTI) as i:
                    for r in range(4):
                        n = 4 * i + r
                        nxt = early(n + 1, r + 1, i) if r < 3 else early(n + 1, 0, i + 1)
                        tile(n, r, nxt, (n - 1, (r - 1) % 4))
                for r in range(4):
                    n = 4 * LASTI + r
                    tile(n, r, early(n + 1, r + 1, LASTI) if r < 3 else None, (n - 1, (r - 1) % 4))
                state(4 * LASTI + 3, 3)

            @block.vector
            def _(dve):
                for s, v in ((d_sa, 1), (d_sb, 1), (d_re, 4), (d_y, 1)):
                    dve.sem_inc(s, v)
                dve.wait_ge(s_cst, 48)
                dve.wait_ge(s_zero, 1)
                dve.tensor_tensor(EM2[:, :], EMU[:, :], EMU[:, :], ALU.mult).then_inc(d_em, 1)
                dve.wait_ge(d_em, 1)
                bd = BD[:, :, :].unsqueeze(1).broadcast_to((P, 2, 4, 32))
                half_decay = lambda z, m, rows=slice(0, P): EMU[rows, ds(z * STEPS + m, 1)]

                def mask(S, bank, k, z):
                    dve.tensor_tensor(S[:, z], PS[:, bank].rearrange("p (h a n) -> p h a n", h=2, a=2),
                                      MSK[:, z, k:k + 2].unsqueeze(1).broadcast_to((P, 2, 2, P)), ALU.mult).then_inc(d_sa if k == 0 else d_sb, 1)

                def early(n, r, m):
                    z = r % 2

                    def a():
                        dve.wait_ge(s_g1, n + 1)
                        mask(SA, 0, 0, z)
                        dve.tensor_scalar(DG[:, z, :], IDN[:, :], half_decay(z, m), None, ALU.mult).then_inc(s_dg, 1)

                    def b():
                        dve.wait_ge(s_g2, n + 1)
                        mask(SB, 1, 2, z)

                    def c():
                        for k, dst in ((0, PX), (1, PT)):
                            last = dve.tensor_tensor(dst[:, z].rearrange("p h (b n) -> p h b n", b=4),
                                                     INV[k][z][:, ds(2 * m, 2), :].unsqueeze(2).broadcast_to((P, 2, 4, 32)), bd, ALU.mult)
                        last.then_inc(d_px, 1)
                    return [a, b, c]

                def add(n, r, k):
                    z = r % 2
                    dve.wait_ge(s_w, 3 * n + k + 1)
                    dve.tensor_tensor(W[:, k % 2], PS[:, 4 - k % 2, 0:2 * P], RH[:, z], ALU.add).then_inc(d_w, 1)

                def finish(n, r, m):
                    z = r % 2
                    dve.wait_ge(s_rey, n + 1)
                    for h in range(2):
                        rows = slice(h * HD, (h + 1) * HD)
                        last = dve.scalar_tensor_tensor(out=RE[rows, z], in0=KX[rows, r, h, 1], scalar=half_decay(z, m, rows),
                                                        in1=PS[rows, 6, h * P:(h + 1) * P], op0=ALU.mult, op1=ALU.add)
                    last.then_inc(d_re, 1)
                    dve.wait_ge(s_at, n + 5)
                    for h in range(2):
                        rows = slice(h * HD, (h + 1) * HD)
                        last = dve.scalar_tensor_tensor(out=ATB[rows, z, rows], in0=IDN[rows, rows], scalar=EM2[rows, ds(z * STEPS + m, 1)],
                                                        in1=PS[rows, 7, rows], op0=ALU.mult, op1=ALU.add)
                    last.then_inc(d_at, 1)

                def yadd(n, r, m):
                    z = r % 2
                    dve.wait_ge(s_h, n + 2)
                    dve.wait_ge(a_y, n + 2)
                    y = Y[z][:, ds(m, 1), :].rearrange("p o n -> p (o n)")
                    dve.tensor_tensor(y, PS[:, 5, 0:P], y, ALU.add).then_inc(d_y, 1)

                def tile(n, r, m, nxt, prev):
                    add(n, r, 0)
                    if nxt: nxt[0]()
                    add(n, r, 1)
                    if prev: yadd(*prev)
                    if nxt: nxt[1]()
                    add(n, r, 2)
                    if nxt: nxt[2]()
                    finish(n, r, m)
                drive(dve, early, tile, lambda n, r, m: yadd(n, r, m))

            @block.scalar
            def _(act):
                for s in (a_rh, a_y, a_h):
                    act.sem_inc(s, 1)
                act.wait_ge(s_cst, 48)

                def early(n, r, m):
                    z = r % 2

                    def a():
                        act.wait_ge(s_mv, n + 1)
                        act.activation(TOK[:, z], PS[:, 2, 2 * P:4 * P], ACT.Copy).then_inc(a_tok, 1)
                        act.activation(RH[:, z], PS[:, 2, 0:2 * P], ACT.Copy).then_inc(a_rh, 1)
                        act.wait_ge(s_zt, n + 1)
                        act.activation(ZT[:, z], PS[:, 3, 0:2 * P], ACT.Copy).then_inc(a_zt, 1)
                    return [a]

                def state(n, r, m):
                    z = r % 2
                    act.wait_ge(s_cst, 48)
                    act.wait_ge(s_h, n + 2)
                    for h in range(2):
                        rows = slice(h * HD, (h + 1) * HD)
                        last = act.activation(HB[rows, z, rows], PS[rows, 7, P + h * HD:P + (h + 1) * HD], ACT.Copy, scale=KEEP[rows, ds(m, 1)])
                    last.then_inc(a_h, 1)

                def tile(n, r, m, nxt, prev):
                    z = r % 2
                    if prev: state(*prev)
                    act.wait_ge(s_wu, n + 3)
                    act.activation(WU[:, z], PS[:, 5, 0:2 * P], ACT.Copy)
                    act.activation(WT[:, z].rearrange("p (a b) -> p a b", b=HD),
                                   PS[:, 5, 0:2 * P].rearrange("p (a b) -> p a b", b=HD)[:, 0:4:3, :], ACT.Copy).then_inc(a_wu, 1)
                    if nxt: nxt[0]()
                    act.wait_ge(d_re, n + 5)
                    act.activation(Y[z][0:HD, ds(m, 1), :].rearrange("p o n -> p (o n)"), PS[HD:P, 6, 0:P], ACT.Copy)
                    act.activation(Y[z][HD:P, ds(m, 1), :].rearrange("p o n -> p (o n)"), PS[0:HD, 6, P:2 * P], ACT.Copy).then_inc(a_y, 1)
                drive(act, early, tile, lambda n, r, m: state(n, r, m))


def finish_layer(nc, sem, PJ, HT, PRM, IDN, PS, prm, WO, GACC, x, b_gate, g_post, consts, out):
    with ExitStack() as st:
        sb = lambda name, shape, dt=F32: st.enter_context(nc.sbuf_tensor(name, shape, dt))
        ROWS = sb("ROWS6", [P, 9, 32])
        SPR = sb("SPR6", [32, 9, P])
        BLK = sb("BLK6", [P, P])
        ONES = sb("ONES6", [P, P])
        RST = sb("RST6", [32, T])
        TG = sb("TG6", [P, 2, T])
        G = sb("G", [P, D])
        GP = sb("GP", [P, D])
        XT = sb("XT", [P, 2, D])
        M = sb("M", [P, 2, D])
        SQ = sb("SQ6", [P, 2, D])
        SS, RS = sb("SS6", [P, 2]), sb("RS6", [P, 2])
        s_cst, s_one, s_gb = sem("consts6_loaded"), sem("ones6_ready"), sem("gate_params_loaded")
        s_gs, d_g = sem("gate_summed"), sem("gate6_ready")
        d_sum, s_mean, d_c, a_sq, s_rows = sem("directions_summed"), sem("means_ready"), sem("centred"), sem("squares6_ready"), sem("variances_summed")
        d_var, a_rst, s_spr, d_gn = sem("variance_inverse"), sem("rstd6_ready"), sem("rstd_spread"), sem("group_normed")
        a_tg, d_tg, d_y, d_mix, s_dve = sem("tanh_gate"), sem("silu_gate"), sem("bonus_added"), sem("mixed_ready"), sem("dve_chain6")
        s_x, s_out = [sem(f"x6_loaded{u}") for u in range(2)], [sem(f"out_stored{u}_plus_16") for u in range(2)]
        s_mm, a_ss, d_v, a_rs, d_m, d_o = sem("tile_projected"), sem("tile_squares"), sem("tile_inverse"), sem("tile_rstd"), sem("tile_scaled"), sem("tile_ready")
        banks = lambda b: PS[:, b:b + 2].rearrange("p a b -> p (a b)")
        MIXED = [GA0 + j for j in range(PAIRS)] + [GR0 + j for j in range(PAIRS)]
        chunks = lambda a: a.rearrange("p (c n) -> p c n", c=TT)
        tokens = lambda a, t: a[ds(t * P, P), :]

        with nc.Block() as block:
            @block.sync
            def _(sp):
                for dst, name, w, rows in ((BLK[:, :], "blocks", P, P), (ROWS[:, :, :].rearrange("p a b -> p (a b)"), "rows", 9 * 32, P),
                                           (SPR[:, :, :].rearrange("p a b -> p (a b)"), "spread", 9 * P, 32)):
                    sp.dma_start(dst, consts[0:rows, CC[name]:CC[name] + w]).then_inc(s_cst, 16)
                sp.dma_start(G[:, :], b_gate.broadcast_to((P, D))).then_inc(s_gb, 16)
                sp.dma_start(GP[:, :], g_post.broadcast_to((P, D))).then_inc(s_gb, 16)
                for u in range(2):
                    sp.sem_inc(s_out[u], 16)
                with sp.Fori(0, TT // 2) as i:
                    for u in range(2):
                        sp.wait_ge(s_out[u], 16 * i + 16)
                        sp.dma_start(XT[:, u], tokens(x, 2 * i + u)).then_inc(s_x[u], 16)
                    for u in range(2):
                        sp.wait_ge(d_o, 2 * i + u + 1)
                        sp.dma_start(tokens(out, 2 * i + u), XT[:, u]).then_inc(s_out[u], 16)
                for u in range(2):
                    sp.wait_ge(s_out[u], 16 * (TT // 2) + 16)

            @block.gpsimd
            def _(pool):
                pool.memset(ONES[:, :], 1.0).then_inc(s_one, 1)

            @block.scalar
            def _(act):
                for j in range(PAIRS):
                    if j >= 2:
                        act.wait_ge(d_tg, j - 1)
                    act.activation(TG[:, j % 2], PJ[:, GR0 + j, :], ACT.Tanh, scale=0.5).then_inc(a_tg, 1)
                    act.wait_ge(d_c, j + 1)
                    act.activation(HT[:, PAIRS + j], HT[:, j], ACT.Square, scale=HD ** -0.5).then_inc(a_sq, 1)
                act.wait_ge(d_var, 1)
                act.activation(RST[:, :], RST[:, :], ACT.Sqrt).then_inc(a_rst, 1)
                with act.Fori(0, TT // 2) as i:
                    for u in range(2):
                        act.wait_ge(s_mm, 2 * i + u + 1)
                        act.activation(SQ[:, u], banks(4 + 2 * u), ACT.Square, scale=D ** -0.5, accum_out=SS[:, u:u + 1]).then_inc(a_ss, 1)
                        act.wait_ge(d_v, 2 * i + u + 1)
                        act.activation(RS[:, u:u + 1], SS[:, u:u + 1], ACT.Sqrt).then_inc(a_rs, 1)

            @block.vector
            def _(dve):
                for j in range(PAIRS):
                    dve.tensor_tensor(chunks(HT[:, j]), chunks(HT[:, j]), chunks(HT[:, PAIRS + j])[:, ORDER[1], :], ALU.add).then_inc(d_sum, 1)
                for j in range(PAIRS):
                    dve.wait_ge(d_sum, j + 1)
                    dve.wait_ge(s_mean, j + 1)
                    dve.scalar_tensor_tensor(out=HT[:, j], in0=banks(0), scalar=-1.0 / HD, in1=HT[:, j], op0=ALU.mult, op1=ALU.add).then_inc(d_c, 1)
                    dve.wait_ge(a_tg, j + 1)
                    dve.scalar_tensor_tensor(out=PJ[:, GR0 + j, :], in0=TG[:, j % 2], scalar=1.0, in1=PJ[:, GR0 + j, :],
                                             op0=ALU.add, op1=ALU.mult).then_inc(d_tg, 1)
                dve.wait_ge(s_rows, 1)
                dve.tensor_scalar(RST[:, :], PS[0:32, 2:4].rearrange("p a b -> p (a b)"), GN_EPS, None, ALU.add).then_inc(s_dve, 1)
                dve.wait_ge(s_dve, 1)
                dve.reciprocal(RST[:, :], RST[:, :]).then_inc(d_var, 1)
                for j in range(PAIRS):
                    dve.wait_ge(s_spr, j + 1)
                    dve.scalar_tensor_tensor(out=HT[:, j], in0=HT[:, j], scalar=prm("gn_w", j), in1=banks(2 * (j % 2)),
                                             op0=ALU.mult, op1=ALU.mult).then_inc(d_gn, 1)
                    dve.wait_ge(d_gn, j + 1)
                    dve.scalar_tensor_tensor(out=HT[:, j], in0=HT[:, j], scalar=prm("gn_b", j), in1=PJ[:, RV0 + j, :],
                                             op0=ALU.add, op1=ALU.add).then_inc(d_y, 1)
                    dve.wait_ge(d_y, j + 1)
                    dve.wait_ge(d_tg, j + 1)
                    dve.scalar_tensor_tensor(out=PJ[:, GR0 + j, :], in0=PJ[:, GR0 + j, :], scalar=0.5, in1=HT[:, j],
                                             op0=ALU.mult, op1=ALU.mult).then_inc(d_mix, 1)
                dve.wait_ge(s_gb, 32)
                dve.wait_ge(s_gs, 1)
                dve.tensor_tensor(G[:, :], banks(0), G[:, :], ALU.add).then_inc(d_g, 1)
                dve.wait_ge(d_g, 1)
                dve.tensor_tensor(G[:, :], G[:, :], GP[:, :], ALU.mult).then_inc(d_g, 1)
                dve.wait_ge(d_g, 2)
                with dve.Fori(0, TT // 2) as i:
                    for u in range(2):
                        n = 2 * i + u + 1
                        dve.wait_ge(a_ss, n)
                        dve.tensor_scalar(SS[:, u:u + 1], SS[:, u:u + 1], NORM_EPS, None, ALU.add).then_inc(s_dve, 1)
                        dve.wait_ge(s_dve, n + 1)
                        dve.reciprocal(SS[:, u:u + 1], SS[:, u:u + 1]).then_inc(d_v, 1)
                        dve.wait_ge(a_rs, n)
                        dve.scalar_tensor_tensor(out=M[:, u], in0=banks(4 + 2 * u), scalar=RS[:, u:u + 1], in1=G[:, :],
                                                 op0=ALU.mult, op1=ALU.mult).then_inc(d_m, 1)
                        dve.wait_ge(d_m, n)
                        dve.wait_ge(s_x[u], 16 * (i + 1))
                        dve.tensor_tensor(XT[:, u], XT[:, u], M[:, u], ALU.add).then_inc(d_o, 1)

            @block.tensor
            def _(pe):
                def project(t, first, last):
                    for k in range(first, last):
                        for half in range(2):
                            m = pe.matmul(PS[:, 4 + 2 * (t % 2) + half], PJ[:, MIXED[k], t * P:(t + 1) * P],
                                          WO[k][:, half * HALF:(half + 1) * HALF], start=(k == 0), stop=(k == KD - 1))
                    return m

                def spread(lhs, rhs, bank):
                    for half in range(2):
                        m = pe.matmul(PS[0:lhs.shape[1], bank + half], lhs, rhs[:, half * HALF:(half + 1) * HALF], start=True, stop=True)
                    return m
                pe.wait_ge(s_cst, 48)
                for j in range(PAIRS):
                    pe.wait_ge(d_sum, j + 1)
                    if j:
                        pe.wait_ge(d_c, j)
                    spread(BLK[:, :], HT[:, j], 0).then_inc(s_mean, 1)
                    project(j // 2, 2 * (j % 2), 2 * (j % 2) + 2)
                for j in range(PAIRS):
                    pe.wait_ge(a_sq, j + 1)
                    for half in range(2):
                        m = pe.matmul(PS[0:32, 2 + half], ROWS[:, j, :], HT[:, PAIRS + j, half * HALF:(half + 1) * HALF],
                                      start=(j == 0), stop=(j == PAIRS - 1))
                m.then_inc(s_rows, 1)
                pe.wait_ge(a_rst, 1)
                for j in range(PAIRS):
                    if j >= 2:
                        pe.wait_ge(d_gn, j - 1)
                    spread(SPR[:, j, :], RST[:, :], 2 * (j % 2)).then_inc(s_spr, 1)
                pe.wait_ge(s_one, 1)
                pe.wait_ge(d_gn, 3)
                spread(ONES[:, :], GACC[:, :], 0).then_inc(s_gs, 1)
                for t in range(TT):
                    if t < 2:
                        for j in range(PAIRS):
                            pe.wait_ge(d_mix, j + 1)
                            m = project(t, PAIRS + j, PAIRS + j + 1)
                    else:
                        pe.wait_ge(d_m, t - 1)
                        m = project(t, 0, KD)
                    m.then_inc(s_mm, 1)


def drive(eng, early, tile, last):
    chunk = lambda i, r: 2 * i + r // 2
    for part in early(0, 0, 0):
        part()
    end = STEPS // 2 - 1

    def four(i, first, final):
        for r in range(4):
            n = 4 * i + r
            nxt = early(n + 1, r + 1, chunk(i, r + 1)) if r < 3 else None if final else early(n + 1, 0, chunk(i + 1, 0))
            prev = None if first and r == 0 else (n - 1, (r - 1) % 4, chunk(i, r - 1) if r else chunk(i - 1, 3))
            tile(n, r, chunk(i, r), nxt, prev)
    four(0, True, False)
    with eng.Fori(1, end) as i:
        four(i, False, False)
    four(end, False, True)
    last(4 * end + 3, 3, chunk(end, 3))


def _columns(v):
    return v.reshape(-1, P).T


def kernel(x, c, w_ada, b_ada, g_pre, w_in, q_norm_g, k_norm_g, shift_taps, w_up, w0, a_up, a0, k_k, k_a, r_k,
           gn_w, gn_b, w_out, g_post):
    import numpy as np
    import concourse.bacc as bacc
    from concourse.bass_utils import run_bass_kernel_spmd

    f = lambda a: np.asarray(a)
    two = lambda v: np.concatenate([v, v])
    parts = {"c": _columns(f(c)[0]), "b_shift": _columns(f(b_ada)[0, :D]), "b_scale": _columns(f(b_ada)[0, D:2 * D]),
             "g_pre": _columns(f(g_pre)[0]),
             "taps": np.concatenate([_columns(f(shift_taps)[0, i]) for i in range(3)], 1),
             "w0": _columns(f(w0)[0].reshape(-1)), "a0": _columns(f(a0)[0].reshape(-1)),
             "k_k": _columns(f(k_k)[0]), "k_a": _columns(f(k_a)[0]), "r_k": _columns(f(r_k)[0].reshape(-1)),
             "gn_w": _columns(f(gn_w)[0]), "gn_b": _columns(f(gn_b)[0]),
             "q_g": two(f(q_norm_g)[0])[:, None], "k_g": two(f(k_norm_g)[0])[:, None]}
    params = np.zeros((P, NPC), np.float32)
    for name, a in parts.items():
        params[:, PC[name]:PC[name] + a.shape[1]] = a
    consts = shape_constants()
    arrays = {"x": f(x)[0], "w_ada": f(w_ada)[0], "w_in": f(w_in)[0], "w_up": f(w_up)[0], "a_up": f(a_up)[0],
              "w_out": f(w_out)[0], "b_gate": f(b_ada)[:, 2 * D:], "g_post": f(g_post), "params": params, "consts": consts}
    arrays = {n: np.ascontiguousarray(a) for n, a in arrays.items()}
    nc = bacc.Bacc("TRN2", target_bir_lowering=False, num_devices=1)
    aps = {n: nc.dram_tensor(f"in_{n}", a.shape, F32, kind="ExternalInput").ap() for n, a in arrays.items()}
    aps["out"] = nc.dram_tensor("out_x", (T, D), F32, kind="ExternalOutput").ap()
    hybrid_layer(nc, **aps)
    r = run_bass_kernel_spmd(nc, [{f"in_{n}": a for n, a in arrays.items()}], core_ids=[0])
    return r.results[0]["out_x"].reshape(1, T, D)


def shape_constants():
    import numpy as np

    k = np.zeros((P, NCC), np.float32)
    i = np.arange(P)
    put = lambda name, a: k[:, CC[name]:CC[name] + a.shape[1]].__setitem__(slice(None), a)
    put("ident", np.eye(P, dtype=np.float32))
    put("blocks", (i[:, None] // HD == i[None, :] // HD).astype(np.float32))
    rot = np.zeros((P, P), np.float32)
    for t in range(P):
        first = t % 32 < 16
        rot[t + 16 if first else t - 16, t] = -1.0 if first else 1.0
    put("rot", rot)
    s, t = i[:, None], i[None, :]
    m = np.zeros((P, 2, 4, P), np.float32)
    for z in range(2):
        a, b = (s, t) if z == 0 else (t, s)
        m[:, z, 0] = (a < b) & (s // 32 != t // 32)
        m[:, z, 1] = m[:, z, 3] = a <= b
        m[:, z, 2] = a < b
    put("mask", m.reshape(P, -1))
    put("bd", (i[:, None] // 32 == i[None, :] // 32).astype(np.float32))
    put("keep", np.broadcast_to((np.arange(STEPS) % TT != TT - 1).astype(np.float32), (P, STEPS)))
    n_freq = HD // 4
    inv = np.float32(10000.0) ** (-np.arange(n_freq, dtype=np.float32) / np.float32(n_freq))
    pos = np.arange(T)
    grid_w = 64
    at = np.where((i % HD < 32)[:, None], (pos // grid_w)[None, :], (pos % grid_w)[None, :]).astype(np.float32)
    ang = at * inv[i % 16][:, None].astype(np.float32)
    put("cos", np.cos(ang).astype(np.float32))
    put("sin", np.sin(ang).astype(np.float32))
    put("start", np.broadcast_to((pos % P != 0).astype(np.float32), (P, T)))
    rows = np.zeros((P, 9, 32), np.float32)
    spread = np.zeros((P, 9, P), np.float32)
    for j in range(9):
        for h in range(2):
            rows[h * HD:(h + 1) * HD, j, 2 * j + h] = 1.0
            spread[2 * j + h, j, h * HD:(h + 1) * HD] = 1.0
    put("rows", rows.reshape(P, -1))
    put("spread", spread.reshape(P, -1))
    put("eps", np.where(i < 2 * PAIRS, L2_EPS, NORM_EPS)[:, None].astype(np.float32))
    return k
```

```python
import concourse.bass as bass
from concourse import mybir
from contextlib import ExitStack

F32 = mybir.dt.float32
F32R = mybir.dt.float32r
ALU = mybir.AluOpType
ACT = mybir.ActivationFunctionType
AXX = mybir.AxisListType.X
ds = bass.ds

P = 128
T = 1024
D = 1024
KD = D // P
TT = T // P
NH = 8
HD = 64
KVH = 2
PAIRS = NH * HD // P
STEPS = PAIRS * TT
RANK = 64
IN_W = 3456
SLOTS = IN_W // P
Q0, K0, V0, GA0, R0, RK0, RV0, WA0, GR0 = 0, 4, 5, 6, 10, 14, 18, 22, 23
ORDER = (slice(None), slice(None, None, -1))
NCONV = 13
DECAY = 0.6065306597126334
NORM_EPS, GN_EPS, L2_EPS = 1e-6, 64e-5, 1e-12
HALF = 512

PC = {}
_n = 0
for _name, _w in (("c", KD), ("b_shift", KD), ("b_scale", KD), ("g_pre", KD), ("taps", 3 * NCONV),
                  ("w0", 2 * PAIRS), ("a0", 2 * PAIRS), ("k_k", PAIRS), ("k_a", PAIRS), ("r_k", PAIRS),
                  ("gn_w", PAIRS), ("gn_b", PAIRS), ("q_g", 1), ("k_g", 1)):
    PC[_name] = _n
    _n += _w
NPC = _n

CC = {}
_n = 0
for _name, _w in (("ident", P), ("blocks", P), ("rot", P), ("rows", 9 * 32), ("mask", 4 * 2 * P), ("bd", P), ("keep", 4 * TT),
                  ("cos", T), ("sin", T), ("start", T), ("spread", 9 * P), ("eps", 1)):
    CC[_name] = _n
    _n += _w
NCC = _n


class Chain:

    def __init__(self, eng, sem, base=0):
        self.eng, self.sem, self.base, self.n = eng, sem, base, 0

    def sig(self, ins):
        self.n += 1
        ins.then_inc(self.sem, 1)
        return self.n

    def upto(self, n):
        self.eng.wait_ge(self.sem, self.base + n)

    def link(self, ins):
        self.upto(self.sig(ins))


def hybrid_layer(nc, x, w_ada, w_in, w_up, a_up, w_out, b_gate, g_post, params, consts, out):
    ctx = ExitStack()
    sb = lambda name, shape, dt=F32: ctx.enter_context(nc.sbuf_tensor(name, shape, dt))
    used = []

    def sem(name):
        used.append(nc.alloc_semaphore(name=name))
        return used[-1]

    def release_semaphores():
        nc.clear_and_free_semaphores(used)
        used.clear()
        nc.all_engine_barrier()

    PJ = sb("PJ", [P, SLOTS, T])
    PRM = sb("PRM", [P, NPC])
    IDN = sb("IDN", [P, P])
    EMU = sb("EMU", [P, 2 * PAIRS * TT])
    CACT = sb("CACT", [P, KD])
    PS = ctx.enter_context(nc.psum_tensor("PS", [P, 8, HALF], F32))
    prm = lambda name, j=0: PRM[:, PC[name] + j:PC[name] + j + 1]

    with ctx:
        start_and_project(nc, sem, PJ, PRM, IDN, CACT, PS, prm, x, w_ada, w_in, params, consts)
        HT = sb("HT", [P, KD, T])
        units = nc.dram_tensor("units", (2, STEPS, P, 5, P), F32).ap()
        norm_and_rotate(nc, sem, PJ, HT, IDN, PS, prm, consts)
        release_semaphores()
        prepare_units(nc, sem, PJ, HT, PRM, EMU, PS, prm, w_up, a_up, consts, units)
        views = [PJ[:, j:j + 4, :].rearrange("p (z a) b -> p z (a b)", z=2).rearrange("p z (g n) -> p z g n", n=32)
                 for j in (RK0, Q0)]
        INV = [[v[:, z] for z in range(2)] for v in views]
        attend(nc, sem, PJ, IDN, PS, INV, units)
        WO7 = sb("WO7", [P, D])
        WO = [PJ[:, j, :] for j in (K0, V0, WA0, R0, R0 + 1, R0 + 2, R0 + 3)] + [WO7[:, :]]
        GACC = sb("GACC", [P, D])
        release_semaphores()
        state_passes(nc, sem, PJ, HT, IDN, EMU, CACT, PS, consts, units, INV, WO, GACC, w_out, w_ada)
        finish_layer(nc, sem, PJ, HT, PS, prm, WO, GACC, x, b_gate, g_post, consts, out)
    return nc


def start_and_project(nc, sem, PJ, PRM, IDN, CACT, PS, prm, x, w_ada, w_in, params, consts):
    with ExitStack() as st:
        sb = lambda name, shape, dt=F32: st.enter_context(nc.sbuf_tensor(name, shape, dt))
        WR = sb("WR", [P, 2, KD, P])
        WH, WL = sb("WH", [P, 2, KD, P], F32R), sb("WL", [P, 2, KD, P], F32R)
        HH, HL = sb("HH", [P, KD, T], F32R), sb("HL", [P, KD, T], F32R)
        HS = PJ[:, 24:26, 0:HALF]
        ACC = sb("ACC", [P, 2 * D])
        ONES = sb("ONES", [P, 1])
        SS = sb("SS", [P, TT])
        RS = sb("RS", [P, TT])
        AM = sb("AM", [P, KD])
        BM = sb("BM", [P, KD])
        X = PJ[:, 0:8, :]
        WA = [PJ[:, 8 + 2 * u:10 + 2 * u, :].rearrange("p a b -> p (a b)") for u in range(8)]
        s_prm, s_x = sem("prm_loaded"), sem("x_loaded")
        s_wada = [sem(f"wada_loaded{k}") for k in range(KD)]
        s_w = [sem(f"w_loaded{u}") for u in range(2)]
        s_dve = sem("dve_chain1")
        s_cact, s_acc, s_mod, s_am = sem("c_act_ready"), sem("acc_ready"), sem("mod_summed"), sem("mod_ready")
        s_ss, s_rs, s_xn = sem("x_squares"), sem("x_rstd"), sem("x_normed")
        s_tr, s_shifted, s_copied = sem("x_transposed"), sem("shifted_tiles_plus_2"), sem("copied_tiles")
        a_hh, d_hs, g_hl, d_hl = sem("h_hi_ready"), sem("h_full_ready"), sem("h_lo_by_pool"), sem("h_lo_by_dve")
        part = lambda a, j: a[:, j % KD, (j // KD) * HALF:(j // KD + 1) * HALF]
        TB = (0, 1, 2, 3, 6, 7)
        a_wh, g_wl = sem("w_hi_ready"), sem("w_lo_ready_plus_2")
        s_mm, s_tap = sem("proj_done_plus_2"), sem("centre_tap_done")

        win = lambda slot: w_in[:, ds(slot * P, P)].rearrange("(k p) n -> p k n", p=P)

        RUNS = [(R0, 6, (1, 1)), (WA0, 1, (1, 0)), (GR0 + 1, 1, (0, 0)), (0, 5, (0, 0))]
        LAST = GR0 + 3

        def pairs(eng, body, runs=RUNS):
            n0 = 0
            for run, (slot0, count, conv) in enumerate(runs):
                if count > 1:
                    with eng.Fori(0, count) as i:
                        for u in range(2):
                            body(n0 + 2 * i + u, slot0 + 2 * i + u, u, conv[u], n0 // 2 + i, run)
                else:
                    for u in range(2):
                        body(n0 + u, slot0 + u, u, conv[u], n0 // 2, run)
                n0 += 2 * count
            if runs is RUNS:
                body(n0, LAST, 0, 0, n0 // 2, len(RUNS))

        with nc.Block() as block:
            @block.sync
            def _(sp):
                sp.dma_start(PRM[:, :], params).then_inc(s_prm, 16)
                sp.dma_start(IDN[:, :], consts[:, CC["ident"]:CC["ident"] + P]).then_inc(s_prm, 16)
                sp.dma_start(X, x.rearrange("(t p) d -> p t d", p=P)).then_inc(s_x, 16)
                for k in range(KD):
                    sp.dma_start(WA[k], w_ada[k * P:(k + 1) * P, 0:2 * D]).then_inc(s_wada[k], 16)

                def load(n, slot, u, conv, k, run):
                    sp.wait_ge(g_wl, n + 1)
                    sp.dma_start(WR[:, u], win(slot)).then_inc(s_w[u], 16)
                pairs(sp, load)

            @block.gpsimd
            def _(pool):
                pool.memset(ONES[:, :], 1.0).then_inc(s_cact, 1)
                pool.sem_inc(g_wl, 2)
                def low(n, u):
                    pool.wait_ge(a_wh, n + 1)
                    pool.tensor_tensor(WL[:, u], WR[:, u], WH[:, u].bitcast(F32), ALU.subtract).then_inc(g_wl, 1)
                low(0, 0)
                for j in range(0, 2 * KD, 2):
                    pool.wait_ge(d_hs, j + 1)
                    pool.tensor_tensor(part(HL, j), HS[:, 0], part(HH, j).bitcast(F32), ALU.subtract).then_inc(g_hl, 1)

                with pool.Fori(0, SLOTS // 2) as k:
                    for u in range(2):
                        low(2 * k + u + 1, 1 - u)

            @block.scalar
            def _(act):
                act.wait_ge(s_prm, 32)
                act.activation(CACT[:, :], PRM[:, PC["c"]:PC["c"] + KD], ACT.Tanh, scale=0.5).then_inc(s_cact, 1)
                act.wait_ge(s_x, 16)
                for t in range(TT):
                    if t >= 3:
                        act.wait_ge(s_ss, t - 2)
                    act.activation(PJ[:, 24 + t % 3, :], X[:, t], ACT.Square, accum_out=SS[:, t:t + 1]).then_inc(s_ss, 1)
                act.wait_ge(s_rs, 1)
                act.activation(RS[:, :], SS[:, :], ACT.Sqrt).then_inc(s_rs, 1)
                act.wait_ge(s_rs, 2)
                for t in range(TT):
                    act.activation(X[:, t], X[:, t], ACT.Copy, scale=RS[:, t:t + 1]).then_inc(s_xn, 1)
                act.wait_ge(s_am, 2)
                def high(n, u, k):
                    act.wait_ge(s_w[u], 16 * (k + 1))
                    act.wait_ge(s_mm, n + 1)
                    act.activation(WH[:, u], WR[:, u], ACT.Copy).then_inc(a_wh, 1)
                high(0, 0, 0)
                for j in range(2 * KD):
                    act.wait_ge(s_tr, j + 1)
                    act.activation(part(HH, j), PS[:, TB[j % 6]], ACT.Identity,
                                   scale=AM[:, j % KD:j % KD + 1], bias=BM[:, j % KD:j % KD + 1]).then_inc(a_hh, 1)

                def evacuate(n, slot, u, conv, k, run):
                    if run < len(RUNS):
                        high(n + 1, 1 - u, k + u)
                    act.wait_ge(s_mm, n + 3)
                    src = PS[:, 4 + 2 * u:6 + 2 * u].rearrange("p a b -> p (a b)")
                    dst = PJ[:, ds(slot, 1), :].rearrange("p a b -> p (a b)")
                    if conv:
                        tap = PRM[:, ds(PC["taps"] + NCONV + (slot - R0), 1)]
                        act.activation(dst, src, ACT.Copy, scale=tap).then_inc(s_tap, 1)
                    else:
                        act.activation(dst, src, ACT.Copy).then_inc(s_copied, 1)
                pairs(act, evacuate)

            @block.vector
            def _(dve):
                chain = Chain(dve, s_dve)
                dve.wait_ge(s_cact, 2)
                chain.link(dve.tensor_scalar(CACT[:, :], CACT[:, :], 1.0, 0.5, ALU.add, ALU.mult))
                chain.link(dve.tensor_tensor(CACT[:, :], CACT[:, :], PRM[:, PC["c"]:PC["c"] + KD], ALU.mult))
                prev = [0, 0]
                for k in range(KD):
                    if k == KD // 2:
                        dve.wait_ge(s_ss, TT)
                        chain.link(dve.tensor_scalar(SS[:, :], SS[:, :], 1.0 / D, NORM_EPS, ALU.mult, ALU.add))
                        dve.reciprocal(SS[:, :], SS[:, :]).then_inc(s_rs, 1)
                    dve.wait_ge(s_wada[k], 16)
                    for h in range(2):
                        a = ACC[:, h * D:(h + 1) * D]
                        w = WA[k][:, h * D:(h + 1) * D]
                        if k == 0:
                            prev[h] = chain.sig(dve.tensor_scalar(a, w, CACT[:, 0:1], None, ALU.mult))
                        else:
                            chain.upto(prev[h])
                            prev[h] = chain.sig(dve.scalar_tensor_tensor(out=a, in0=w, scalar=CACT[:, k:k + 1], in1=a,
                                                                         op0=ALU.mult, op1=ALU.add))
                chain.upto(prev[1])
                dve.sem_inc(s_acc, 1)
                dve.wait_ge(s_mod, 1)
                chain.link(dve.tensor_tensor(AM[:, :], PS[:, 4, KD:2 * KD], PRM[:, PC["b_scale"]:PC["b_scale"] + KD], ALU.add))
                dve.scalar_tensor_tensor(out=AM[:, :], in0=AM[:, :], scalar=1.0, in1=PRM[:, PC["g_pre"]:PC["g_pre"] + KD],
                                         op0=ALU.add, op1=ALU.mult).then_inc(s_am, 1)
                dve.tensor_tensor(BM[:, :], PS[:, 4, 0:KD], PRM[:, PC["b_shift"]:PC["b_shift"] + KD], ALU.add).then_inc(s_am, 1)
                dve.wait_ge(s_am, 2)
                for j in range(2 * KD):
                    dve.wait_ge(a_hh, j + 1)
                    if j >= 2:
                        dve.wait_ge(g_hl if j % 2 == 0 else d_hl, j // 2)
                    dve.tensor_scalar(HS[:, j % 2], PS[:, TB[j % 6]], AM[:, j % KD:j % KD + 1],
                                      BM[:, j % KD:j % KD + 1], ALU.mult, ALU.add).then_inc(d_hs, 1)
                    if j % 2:
                        dve.wait_ge(d_hs, j + 1)
                        dve.tensor_tensor(part(HL, j), HS[:, 1], part(HH, j).bitcast(F32), ALU.subtract).then_inc(d_hl, 1)
                def taps(n, slot, u, conv, k, run):
                    if not conv:
                        return
                    dve.wait_ge(s_tap, n + 1)
                    src = PS[:, 4 + 2 * u:6 + 2 * u].rearrange("p a b -> p (a b)")
                    dst = PJ[:, ds(slot, 1), :].rearrange("p a b -> p (a b)")
                    left = PRM[:, ds(PC["taps"] + (slot - R0), 1)]
                    right = PRM[:, ds(PC["taps"] + 2 * NCONV + (slot - R0), 1)]
                    dve.scalar_tensor_tensor(out=dst[:, 1:T], in0=src[:, 0:T - 1], scalar=left, in1=dst[:, 1:T],
                                             op0=ALU.mult, op1=ALU.add).then_inc(s_dve, 1)
                    dve.wait_ge(s_dve, chain.n + n + 1)
                    dve.scalar_tensor_tensor(out=dst[:, 0:T - 1], in0=src[:, 1:T], scalar=right, in1=dst[:, 0:T - 1],
                                             op0=ALU.mult, op1=ALU.add).then_inc(s_shifted, 1)
                pairs(dve, taps, RUNS[:2])

            @block.tensor
            def _(pe):
                pe.sem_inc(s_mm, 2)
                pe.wait_ge(s_acc, 1)
                for j in range(2 * KD):
                    m = pe.matmul(PS[:, 4, j:j + 1], ACC[:, j * P:(j + 1) * P], ONES[:, 0:1], start=True, stop=True)
                m.then_inc(s_mod, 1)
                pe.wait_ge(s_xn, TT)
                for j in range(2 * KD):
                    if j >= 6:
                        pe.wait_ge(d_hs, j - 5)
                    for t in range(4):
                        m = pe.transpose(PS[:, TB[j % 6], t * P:(t + 1) * P],
                                         X[:, (j // KD) * 4 + t, (j % KD) * P:(j % KD + 1) * P], IDN[:, :])
                    m.then_inc(s_tr, 1)

                pe.sem_inc(s_shifted, 2)
                def project(n, slot, u, conv, k, run):
                    pe.wait_ge(g_wl, n + 3)
                    if run < 2 or (run == 2 and u == 0):
                        pe.wait_ge(s_shifted, n + 1)
                    else:
                        pe.wait_ge(s_copied, n - (NCONV + 1))
                    for half in range(2):
                        pe.wait_ge(g_hl, KD // 2 * (half + 1))
                        pe.wait_ge(d_hl, KD // 2 * (half + 1))
                        for kk in range(KD):
                            for term, (w, h) in enumerate(((WH, HH), (WH, HL), (WL, HH))):
                                m = pe.matmul(PS[:, 4 + 2 * u + half], w[:, u, kk, :], h[:, kk, half * HALF:(half + 1) * HALF],
                                              start=(kk == 0 and term == 0), stop=(kk == KD - 1 and term == 2))
                    m.then_inc(s_mm, 1)
                pairs(pe, project)



def norm_and_rotate(nc, sem, PJ, HT, IDN, PS, prm, consts):
    with ExitStack() as st:
        sb = lambda name, shape, dt=F32: st.enter_context(nc.sbuf_tensor(name, shape, dt))
        KK = HT[:, 0:4, :]
        VT = HT[:, 4:8, :].rearrange("p a b -> p (a b)").rearrange("p (c n) -> p c n", c=TT)
        ROT = sb("ROT", [P, P])
        ROWS = sb("ROWS", [P, 9, 32])
        SPE = sb("SPE", [P, 9 * P + 1])
        SPR, EPS = SPE[:, 0:9 * P].rearrange("p (j m) -> p j m", m=P), SPE[:, 9 * P:9 * P + 1]
        CS = sb("CS", [P, 2, T])
        SQ = sb("SQ", [P, 4, T])
        QC = sb("QC", [P, 2, T])
        QS = sb("QS", [P, T])
        RST = sb("RST", [P, T])

        s_cst, s_wa, s_vt, s_vtc = sem("consts2_loaded"), sem("wd_tanh"), sem("v_transposed"), sem("v_copied")
        s_sq, s_sums, s_var, s_rst = sem("squares_ready"), sem("sums_of_squares"), sem("inverse_squares"), sem("inverse_norms")
        s_spr, s_unit, s_rot, s_cosd, s_roped = sem("norms_spread"), sem("normed"), sem("rotated"), sem("times_cos"), sem("roped")
        s_dve, s_rz = sem("dve_chain2"), sem("rst_zeroed")
        slot = lambda j: PJ[:, j, :]
        source = lambda j: slot(RK0 + j) if j < 4 else slot(Q0 + j - 4)
        banks = lambda b: PS[:, b:b + 2].rearrange("p a b -> p (a b)")

        with nc.Block() as block:
            @block.sync
            def _(sp):
                for dst, name, w, rows in ((ROWS[:, :, :].rearrange("p a b -> p (a b)"), "rows", 9 * 32, P), (ROT[:, :], "rot", P, P),
                                           (SPE[:, :], "spread", 9 * P + 1, P), (CS[:, 0], "cos", T, P), (CS[:, 1], "sin", T, P)):
                    sp.dma_start(dst, consts[0:rows, CC[name]:CC[name] + w]).then_inc(s_cst, 16)

            @block.gpsimd
            def _(pool):
                pool.memset(RST[:, :], 0.0).then_inc(s_rz, 1)
                pool.wait_ge(s_cst, 80)
                for j in range(5):
                    pool.wait_ge(s_unit, 4 + j + 1)
                    if j >= 2:
                        pool.wait_ge(s_roped, j - 1)
                    pool.tensor_tensor(QC[:, j % 2], slot(Q0 + j), CS[:, 0], ALU.mult).then_inc(s_cosd, 1)

            @block.scalar
            def _(act):
                act.activation(PJ[0:RANK, WA0, :], PJ[0:RANK, WA0, :], ACT.Tanh).then_inc(s_wa, 1)
                for j in range(9):
                    if j >= 4:
                        act.wait_ge(s_sums, j - 3)
                    act.activation(SQ[:, j % 4], source(j), ACT.Square, scale=prm("k_k", j) if j < 4 else HD ** -0.5).then_inc(s_sq, 1)
                for c in range(TT):
                    act.wait_ge(s_vt, c + 1)
                    act.activation(VT[:, c, :], PS[:, 6 + c % 2], ACT.Copy).then_inc(s_vtc, 1)
                act.wait_ge(s_var, 1)
                act.activation(RST[0:32, :], RST[0:32, :], ACT.Sqrt).then_inc(s_rst, 1)

            @block.vector
            def _(dve):
                chain = Chain(dve, s_dve)
                dve.wait_ge(s_cst, 80)
                dve.wait_ge(s_rz, 1)
                dve.wait_ge(s_sums, 9)
                chain.link(dve.tensor_scalar(RST[0:32, :], PS[0:32, 0:2].rearrange("p a b -> p (a b)"), EPS[0:32, 0:1], None, ALU.add))
                dve.reciprocal(RST[0:32, :], RST[0:32, :]).then_inc(s_var, 1)

                def rope(j):
                    dve.wait_ge(s_rot, j + 1)
                    chain.link(dve.tensor_tensor(QS[:, :], banks(6), CS[:, 1], ALU.mult))
                    dve.wait_ge(s_cosd, j + 1)
                    dve.tensor_tensor(slot(Q0 + j), QC[:, j % 2], QS[:, :], ALU.add).then_inc(s_roped, 1)

                for j in range(9):
                    dve.wait_ge(s_spr, j + 1)
                    g = prm("k_k", j) if j < 4 else prm("q_g") if j < 8 else prm("k_g")
                    dst = KK[:, j] if j < 4 else source(j)
                    dve.scalar_tensor_tensor(out=dst, in0=source(j), scalar=g, in1=banks(2 + 2 * (j % 2)),
                                             op0=ALU.mult, op1=ALU.mult).then_inc(s_unit, 1)
                    if j >= 5:
                        rope(j - 5)
                rope(4)

            @block.tensor
            def _(pe):
                pe.wait_ge(s_cst, 80)
                for j in range(9):
                    pe.wait_ge(s_sq, j + 1)
                    for half in range(2):
                        m = pe.matmul(PS[0:32, half], ROWS[:, j, :], SQ[:, j % 4, half * HALF:(half + 1) * HALF],
                                      start=(j == 0), stop=(j == 8))
                    m.then_inc(s_sums, 1)
                for c in range(TT):
                    if c >= 2:
                        pe.wait_ge(s_vtc, c - 1)
                    for p in range(PAIRS):
                        m = pe.transpose(PS[:, 6 + c % 2, p * P:(p + 1) * P], PJ[:, RV0 + p, c * P:(c + 1) * P], IDN[:, :])
                    m.then_inc(s_vt, 1)
                pe.wait_ge(s_rst, 1)
                pe.wait_ge(s_vtc, TT)

                def rotate(j):
                    pe.wait_ge(s_unit, 4 + j + 1)
                    if j >= 1:
                        pe.wait_ge(s_roped, j)
                    for half in range(2):
                        m = pe.matmul(PS[:, 6 + half], ROT[:, :], PJ[:, Q0 + j, half * HALF:(half + 1) * HALF], start=True, stop=True)
                    m.then_inc(s_rot, 1)

                for j in range(9):
                    if j >= 2:
                        pe.wait_ge(s_unit, j - 1)
                    for half in range(2):
                        m = pe.matmul(PS[:, 2 + 2 * (j % 2) + half], SPR[:, j, :], RST[:, half * HALF:(half + 1) * HALF], start=True, stop=True)
                    m.then_inc(s_spr, 1)
                    if j >= 5:
                        rotate(j - 5)
                rotate(4)


def prepare_units(nc, sem, PJ, HT, PRM, EMU, PS, prm, w_up, a_up, consts, units):
    with ExitStack() as st:
        sb = lambda name, shape, dt=F32: st.enter_context(nc.sbuf_tensor(name, shape, dt))
        KK = HT[:, 0:4, :]
        VT = HT[:, 4:8, :].rearrange("p a b -> p (a b)").rearrange("p (c n) -> p c n", c=TT)
        BLK = sb("BLK", [P, P])
        START = sb("START", [P, T])
        UP = sb("UP", [P, 2, 2, P])
        KAC = sb("KAC", [P, PAIRS])
        TW = sb("TW", [P, 2, T])
        TA = sb("TA", [P, 2, T])
        FF = sb("FF", [P, 2, T])
        MU = sb("MU", [P, 2, TT])
        OB = sb("OB", [P, 2, 4, T])
        CHAIN = 4

        s_cst, s_zero, s_up, s_pre = sem("consts3_loaded"), sem("up_zeroed"), [sem("up_loaded0"), sem("up_loaded1")], sem("pre_activations_plus_2")
        s_tw, s_ta, s_g, s_e = sem("tanh_w"), sem("tanh_a_plus_1"), sem("exponents_ready"), [sem(f"exp{k}_ready") for k in range(3)]
        s_u, s_kt, s_kq, s_rr, s_ai, s_ki = (sem(n) for n in ("u_ready", "kt_ready", "kq_ready", "rr_ready", "ai_ready_plus_2", "ki_ready"))
        s_st = [sem(f"stored{z}_plus_16") for z in range(2)]
        s_vst, s_ak = sem("v_stored"), sem("a_kk_ready")
        s_prod, s_bsum, s_bon, s_dve, s_hp, s_mu = sem("bonus_product"), sem("bonus_summed_plus_2"), sem("bonus_ready_plus_1"), sem("dve_chain3"), sem("halves_ready"), sem("emu_ready_plus_2")
        dyn = lambda a, j: a[:, ds(j, 1), :].rearrange("p a b -> p (a b)")
        banks = lambda b: PS[:, b:b + 2].rearrange("p a b -> p (a b)")
        chunks = lambda a: a.rearrange("p (c n) -> p c n", c=TT)

        def in_turn(eng, begin, end):
            begin(0, 0)
            with eng.Fori(0, PAIRS - 1) as p:
                begin(p, 1)
                end(p, 0)
                begin(p + 1, 0)
                end(p, 1)
            begin(PAIRS - 1, 1)
            end(PAIRS - 1, 0)
            end(PAIRS - 1, 1)

        with nc.Block() as block:
            @block.sync
            def _(sp):
                sp.dma_start(BLK[:, :], consts[:, CC["blocks"]:CC["blocks"] + P]).then_inc(s_cst, 16)
                sp.dma_start(START[:, :], consts[:, CC["start"]:CC["start"] + T]).then_inc(s_cst, 16)
                for z in range(2):
                    for p in range(PAIRS):
                        sp.dma_start(units[z, p * TT:(p + 1) * TT, :, 4, :].rearrange("c p n -> p c n"),
                                     VT[:, ORDER[z], p * P:(p + 1) * P]).then_inc(s_vst, 16)
                for z in range(2):
                    sp.sem_inc(s_st[z], 16)

                def store(p, z):
                    for a, s_a, more in ((0, s_kq, 0), (3, s_ki, 0), (2, s_ai, 2), (1, s_rr, 0)):
                        sp.wait_ge(s_a, 2 * p + z + 1 + more)
                        sp.dma_start(units[z, ds(p * TT, TT), :, a, :].rearrange("c p n -> p c n"),
                                     chunks(OB[:, z, a])[:, ORDER[z], :]).then_inc(s_st[z], 16)
                in_turn(sp, lambda p, z: None, store)
                for z in range(2):
                    sp.wait_ge(s_st[z], 64 * PAIRS + 16)
                sp.wait_ge(s_vst, 16 * 2 * PAIRS)

            @block.gpsimd
            def _(pool):
                pool.memset(UP[:, :, :, :], 0.0).then_inc(s_zero, 1)
                for n in range(2 * PAIRS):
                    p, z = n // 2, n % 2
                    pool.wait_ge(s_u, n + 1)
                    pool.tensor_tensor(OB[:, z, 3], OB[:, z, 3], PJ[:, RK0 + p, :], ALU.mult).then_inc(s_kt, 1)
                    pool.wait_ge(s_e[0], n + 1)
                    pool.tensor_tensor(OB[:, z, 0], OB[:, z, 0], KK[:, p], ALU.mult).then_inc(s_kq, 1)
                    pool.wait_ge(s_e[1], n + 1)
                    pool.tensor_tensor(OB[:, z, 1], OB[:, z, 1], PJ[:, R0 + p, :], ALU.mult).then_inc(s_rr, 1)

            @block.scalar
            def _(act):
                act.sem_inc(s_ta, 1)
                act.sem_inc(s_mu, 2)
                act.wait_ge(s_hp, 1)
                act.wait_ge(s_zero, 1)

                def load(p, z):
                    act.dma_start(UP[0:RANK, z, 0, :], w_up[z, :, ds(p * P, P)]).then_inc(s_up[z], 16)
                    act.dma_start(UP[RANK:P, z, 1, :], a_up[z, :, ds(p * P, P)]).then_inc(s_up[z], 16)
                for z in range(2):
                    load(0, z)

                def rates(p, z):
                    n = 2 * p + z + 1
                    act.wait_ge(s_pre, n + 2)
                    if not isinstance(p, int):
                        load(p + z, 1 - z)
                    act.wait_ge(s_mu, n)
                    act.activation(TW[:, z], banks(0), ACT.Tanh, scale=0.5, bias=PRM[:, ds(PC["w0"] + PAIRS * z + p, 1)]).then_inc(s_tw, 1)
                    act.wait_ge(s_ai, n)
                    act.activation(TA[:, z], banks(2), ACT.Tanh, scale=0.5, bias=PRM[:, ds(PC["a0"] + PAIRS * z + p, 1)]).then_inc(s_ta, 1)

                def exponents(p, z):
                    act.wait_ge(s_ta, 2 * p + z + 2)
                    act.wait_ge(s_st[z], 64 * p + 16)
                    act.wait_ge(s_g, 2 * p + z + 1)
                    incl, excl = (FF, TW) if z == 0 else (TW, FF)
                    act.activation(OB[:, z, 0], excl[:, z], ACT.Exp).then_inc(s_e[0], 1)
                    act.activation(OB[:, z, 3], TA[:, z], ACT.Identity, scale=PRM[:, ds(PC["k_a"] + p, 1)],
                                   bias=KAC[:, ds(p, 1)]).then_inc(s_u, 1)
                    act.activation(OB[:, z, 2], incl[:, z], ACT.Exp, scale=-1.0).then_inc(s_e[2], 1)
                    act.activation(OB[:, z, 1], incl[:, z], ACT.Exp).then_inc(s_e[1], 1)
                    act.activation(EMU[:, ds((PAIRS * z + p) * TT, TT)], MU[:, z, ORDER[z]], ACT.Exp).then_inc(s_mu, 1)
                in_turn(act, rates, exponents)

            @block.vector
            def _(dve):
                chain = Chain(dve, s_dve)
                w = PC["a0"] + 2 * PAIRS
                halves = PRM[:, PC["w0"]:w]
                dve.tensor_scalar(halves, halves, 0.5, None, ALU.mult).then_inc(s_dve, 1)
                ka = PRM[:, PC["k_a"]:PC["k_a"] + PAIRS]
                dve.tensor_scalar(ka, ka, 0.5, None, ALU.mult).then_inc(s_dve, 1)
                dve.wait_ge(s_dve, 2)
                dve.tensor_scalar(KAC[:, :], ka, -1.0, 1.0, ALU.mult, ALU.add).then_inc(s_hp, 1)
                dve.wait_ge(s_hp, 1)
                dve.wait_ge(s_cst, 32)
                dve.sem_inc(s_ai, 2)
                dve.sem_inc(s_bon, 1)

                def decays(p, z):
                    n = 2 * p + z + 1
                    chain.base, chain.n = 2 + CHAIN * (n - 1), 0
                    dve.wait_ge(s_tw, n)
                    chain.link(dve.tensor_scalar(TW[:, z], TW[:, z], 1.0, -0.5 * DECAY, ALU.add, ALU.mult))
                    dve.wait_ge(s_bsum, n)
                    chain.link(dve.tensor_tensor_scan(FF[:, z], START[:, :], TW[:, z], 0.0, ALU.mult, ALU.add))
                    dve.wait_ge(s_mu, n)
                    chain.link(dve.tensor_scalar(MU[:, z, :], chunks(FF[:, z])[:, :, P - 1], 0.5, None, ALU.mult))
                    mu = MU[:, z, :].unsqueeze(2).broadcast_to((P, TT, P))
                    a, b = (chunks(FF[:, z]), mu) if z == 0 else (mu, chunks(FF[:, z]))
                    chain.link(dve.tensor_tensor(chunks(FF[:, z]), a, b, ALU.subtract))
                    dve.tensor_tensor(TW[:, z], FF[:, z], TW[:, z], ALU.subtract if z == 0 else ALU.add).then_inc(s_g, 1)
                    assert chain.n == CHAIN

                def outputs(p, z):
                    n = 2 * p + z + 1
                    dve.wait_ge(s_kt, n)
                    dve.wait_ge(s_e[1], n)
                    dve.scalar_tensor_tensor(out=FF[:, z], in0=dyn(PJ, R0 + p), scalar=PRM[:, ds(PC["r_k"] + p, 1)],
                                             in1=OB[:, z, 3], op0=ALU.mult, op1=ALU.mult).then_inc(s_prod, 1)
                    dve.wait_ge(s_u, n)
                    dve.scalar_tensor_tensor(out=TA[:, z], in0=TA[:, z], scalar=1.0, in1=dyn(KK, p),
                                             op0=ALU.add, op1=ALU.mult).then_inc(s_ak, 1)
                    dve.wait_ge(s_prod, n)
                    dve.tensor_tensor(OB[:, z, 3], OB[:, z, 3], OB[:, z, 2], ALU.mult).then_inc(s_ki, 1)
                    dve.wait_ge(s_ak, n)
                    dve.wait_ge(s_ki, n)
                    dve.scalar_tensor_tensor(out=OB[:, z, 2], in0=TA[:, z], scalar=-0.5, in1=OB[:, z, 2],
                                             op0=ALU.mult, op1=ALU.mult).then_inc(s_ai, 1)
                    if z == 1:
                        dve.wait_ge(s_bsum, n + 2)
                        dve.tensor_tensor(dyn(PJ, RV0 + p), banks(4), dyn(PJ, RV0 + p), ALU.mult).then_inc(s_bon, 1)
                in_turn(dve, decays, outputs)

            @block.tensor
            def _(pe):
                pe.sem_inc(s_pre, 2)
                pe.wait_ge(s_cst, 32)

                pe.sem_inc(s_bsum, 2)

                def pre(p, z):
                    pe.wait_ge(s_up[z], 32 * (p + 1))
                    pe.wait_ge(s_ta, 2 * p + z + 1)
                    for k in range(2):
                        for half in range(2):
                            m = pe.matmul(PS[:, 2 * k + half], UP[:, z, k, :], PJ[:, WA0, half * HALF:(half + 1) * HALF],
                                          start=True, stop=True)
                    m.then_inc(s_pre, 1)

                def bonus(p, z):
                    pe.wait_ge(s_prod, 2 * p + z + 1)
                    if z == 0:
                        pe.wait_ge(s_bon, p + 1)
                    for half in range(2):
                        m = pe.matmul(PS[:, 4 + half], BLK[:, :], FF[:, z, half * HALF:(half + 1) * HALF],
                                      start=(z == 0), stop=(z == 1))
                    m.then_inc(s_bsum, 1)
                for z in range(2):
                    pre(0, z)
                with pe.Fori(0, PAIRS - 1) as p:
                    for z in range(2):
                        pre(p + 1, z)
                        bonus(p, z)
                for z in range(2):
                    bonus(PAIRS - 1, z)


def block_views(PJ):
    flat = lambda j: PJ[:, j:j + 4, :].rearrange("p a b -> p (a b)")
    nd = flat(R0).rearrange("p (z g t) -> p z g t", z=2, t=32)
    return [nd[:, 0], nd[:, 1]], PJ[:, RK0:RK0 + 4, :]


def attend(nc, sem, PJ, IDN, PS, INV, units):
    with ExitStack() as st:
        sb = lambda name, shape, dt=F32: st.enter_context(nc.sbuf_tensor(name, shape, dt))
        KHL = sb("KHL", [P, KVH, T], F32R)
        QH, QL = sb("QH", [P, 2, T], F32R), sb("QL", [P, 2, T], F32R)
        VA = sb("VA", [P, KVH, TT, P])
        ONE = sb("ONE", [P, P], F32R)
        PB = sb("PB", [P, 2, HALF])
        MX = sb("MX", [P, 2])
        DG = sb("DGM", [P, 2, HALF], F32R)
        TG = sb("TG", [P, T])
        RD = sb("RD", [HD, HALF])
        NX = sb("NX", [P, HALF])
        TMP = sb("TMP", [P, 4, 16 * 17])
        KX = sb("KX1", [P, 2, 4, 2, P])
        AI = sb("AI1", [P, 2, 4, P])

        ND, NT = block_views(PJ)
        s_zero, s_ld = sem("kx_zeroed"), [sem(f"products_loaded{z}") for z in range(2)]
        s_g, a_nd, d_nt = sem("products_done_plus_4"), sem("blocks_taken_plus_2"), sem("blocks_turned")
        XS = PJ[:, R0:R0 + 4, :].rearrange("p b (i c) -> p b i c", c=32)
        s_vtr, a_va, a_va2, d_one = sem("va_transposed"), sem("va_ready_plus_2"), sem("two_ready"), sem("one_ready")
        a_kh, d_kl = sem("k_hi_ready"), sem("k_lo_ready")
        a_qh, d_ql = sem("q_hi_ready"), sem("q_lo_ready")
        s_s, d_mx, d_dg = sem("scores_ready"), sem("max_ready_plus_1"), sem("minus_max_ready")
        s_st, a_p, s_pv, d_o = sem("scores_t_ready_plus_32"), sem("weights_ready_plus_2"), sem("outputs_summed_plus_2"), sem("output_taken_plus_2")
        a_tg, d_gate, d_rd, d_nx = sem("gate_tanh"), sem("gate_ready_plus_1"), sem("rden_ready"), sem("normalised")
        g_sub, d_inv = sem("pool_chain"), sem("inverses_turned")
        banks = lambda b: PS[:, b:b + 2].rearrange("p a b -> p (a b)")
        dyn = lambda j, rows=slice(0, P): PJ[rows, ds(j, 1), :].rearrange("p a b -> p (a b)")
        half_rows = lambda h: slice(h * HD, (h + 1) * HD)

        with nc.Block() as block:
            @block.sync
            def _(sp):
                sp.wait_ge(s_zero, 1)
                with sp.Fori(0, STEPS // 4) as i:
                    for z in range(2):
                        sp.wait_ge(s_g, 4 * i + 2 * z + 2)
                        group = units[z, ds(4 * i, 4)]
                        for h in range(2):
                            sp.dma_start(KX[half_rows(h), z, :, h, :], group[:, half_rows(h), 0, :].rearrange("m p n -> p m n")).then_inc(s_ld[z], 16)
                        sp.dma_start(AI[:, z], group[:, :, 2, :].rearrange("m p n -> p m n")).then_inc(s_ld[z], 16)

            @block.gpsimd
            def _(pool):
                pool.memset(KX[:, :, :, :, :], 0.0).then_inc(s_zero, 1)
                pool.memset(VA[:, :, :, HD:P], 2.0).then_inc(a_va2, 1)
                chain = Chain(pool, g_sub)
                pool.wait_ge(d_nt, 4)
                chain.link(pool.memset(XS, 0.0))
                chain.link(pool.memset(PJ[:, R0:R0 + 4, 0:T:33], 1.0))
                nt = NT.rearrange("p b (i j) -> p b i j", j=32)
                for j in range(31):
                    low, left = 31 - j, j + 1
                    t = TMP[:, :, 0:low * left].rearrange("p b (i c) -> p b i c", c=left)
                    n_col = nt[:, :, j + 1:32, j].unsqueeze(3).broadcast_to((P, 4, low, left))
                    x_row = XS[:, :, j, 0:left].unsqueeze(2).broadcast_to((P, 4, low, left))
                    chain.link(pool.tensor_tensor(t, n_col, x_row, ALU.mult))
                    dst = XS[:, :, j + 1:32, 0:left]
                    chain.link(pool.tensor_tensor(dst, dst, t, ALU.add))

            @block.scalar
            def _(act):
                for kv in range(KVH):
                    act.activation(KHL[half_rows(kv), kv], PJ[half_rows(kv), K0, :], ACT.Copy).then_inc(a_kh, 1)
                act.sem_inc(a_va, 2)
                for c in range(TT):
                    act.wait_ge(s_vtr, c + 1)
                    act.activation(VA[:, :, c, 0:HD], PS[:, 4 + c % 2, 0:P].rearrange("p (a b) -> p a b", a=2), ACT.Copy).then_inc(a_va, 1)
                act.sem_inc(a_p, 2)
                act.sem_inc(a_nd, 2)

                def high(p, h, part):
                    if part == 0:
                        act.wait_ge(s_st, 16 * (2 * p + h + 1))
                    last = act.activation(QH[half_rows(part), h], dyn(Q0 + p, half_rows(h)), ACT.Copy)
                    if part == 1:
                        last.then_inc(a_qh, 1)
                for part in range(2):
                    high(0, 0, part)

                def pair(p, kv, final=False):
                    for u in range(4):
                        for k in range(TT):
                            g = 8 * (4 * p + u) + k
                            act.wait_ge(s_st, g + 33)
                            act.wait_ge(s_pv, g + 1)
                            act.activation(PB[:, k % 2], PS[:, 4 + k % 2], ACT.Exp, scale=HD ** -0.5).then_inc(a_p, 1)
                            if u == 0 and k < 2:
                                high(p, 1, k)
                            if u == 0 and k == 2:
                                act.wait_ge(d_gate, p + 1)
                                act.activation(TG[:, :], dyn(GA0 + p), ACT.Tanh, scale=0.5).then_inc(a_tg, 1)
                            if u == 2 and k < 2 and not final:
                                high(p + 1, 0, k)
                            if kv == 0 and k % 2:
                                act.wait_ge(s_g, 4 * (4 * p + u) + k // 2 + 5)
                                for q in range(4):
                                    rows = slice(32 * q, 32 * q + 32)
                                    last = act.activation(ND[k // 4][rows, ds(8 * (4 * p + u) + 2 * (k - 1) % 8, 4), :],
                                                          PS[rows, 2 + k // 2 % 2, :].rearrange("p (g n) -> p g n", n=P)[:, :, 32 * q:32 * q + 32], ACT.Copy)
                                last.then_inc(a_nd, 1)
                with act.Fori(0, PAIRS // KVH) as p:
                    pair(p, 0)
                pair(PAIRS - 2, 1)
                pair(PAIRS - 1, 1, final=True)

            @block.vector
            def _(dve):
                dve.tensor_scalar(ONE[:, :], IDN[:, :], 0.0, 1.0, ALU.mult, ALU.add).then_inc(d_one, 1)
                for kv in range(KVH):
                    r = half_rows(kv)
                    dve.wait_ge(a_kh, kv + 1)
                    dve.tensor_tensor(KHL[half_rows(1 - kv), kv], PJ[r, K0, :], KHL[r, kv].bitcast(F32), ALU.subtract).then_inc(d_kl, 1)
                dve.sem_inc(d_mx, 1)
                dve.sem_inc(d_o, 2)
                dve.sem_inc(d_gate, 1)
                dve.wait_ge(d_one, 1)

                def lows(p, h):
                    dve.wait_ge(a_qh, 2 * p + h + 1)
                    for part in range(2):
                        last = dve.tensor_tensor(QL[half_rows(part), h], dyn(Q0 + p, half_rows(h)), QH[half_rows(h), h].bitcast(F32), ALU.subtract)
                    last.then_inc(d_ql, 1)

                def maxima(p, u, between=(), wide=False):
                    dve.wait_ge(s_st, 8 * (4 * p + u) + 24)
                    for t in range(4):
                        if t >= 2 and between:
                            between[t - 2]()
                        c = 4 * (4 * p + u) + t
                        dve.wait_ge(s_s, c + 1)
                        dve.reduce_max(MX[:, t % 2:t % 2 + 1], banks(2 * (t % 2) if wide else 0), AXX).then_inc(d_mx, 1)
                        dve.wait_ge(d_mx, c + 2)
                        dve.tensor_scalar(DG[:, u % 2, t * P:(t + 1) * P], IDN[:, :], MX[:, t % 2:t % 2 + 1], -1.0,
                                          ALU.mult, ALU.mult).then_inc(d_dg, 1)

                def finish(p, u):
                    n, r, cols = 4 * p + u, half_rows(u // 2), slice((u % 2) * HALF, (u % 2 + 1) * HALF)
                    dve.wait_ge(s_pv, 8 * n + 10)
                    dve.reciprocal(RD[:, :], PS[HD:P, 6 + u % 2]).then_inc(d_rd, 1)
                    dve.wait_ge(d_rd, n + 1)
                    dve.tensor_tensor(NX[r, :], PS[0:HD, 6 + u % 2], RD[:, :], ALU.mult).then_inc(d_o, 1)
                    dve.wait_ge(d_o, n + 3)
                    o = dyn(GA0 + p, r)[:, cols]
                    dve.tensor_tensor(o, o, NX[r, :], ALU.mult).then_inc(d_nx, 1)

                def gate(p):
                    dve.wait_ge(a_tg, p + 1)
                    dve.scalar_tensor_tensor(out=dyn(GA0 + p), in0=TG[:, :], scalar=1.0, in1=dyn(GA0 + p),
                                             op0=ALU.add, op1=ALU.mult).then_inc(d_gate, 1)

                def turn_inverses():
                    dve.wait_ge(g_sub, 2 + 2 * 31)
                    for z in range(2):
                        for half in range(2):
                            x = XS[:, 2 * z + half]
                            by_row, by_col = x.rearrange("p i c -> p c i"), x
                            if z == 1:
                                by_row, by_col = by_col, by_row
                            for k, src in ((0, by_row), (1, by_col)):
                                dst = INV[k][z][:, 32 * half:32 * half + 32, :].rearrange("p g n -> p n g")
                                dve.transpose(dst, src).then_inc(d_inv, 1)

                def pair(p, wide=False, final=False):
                    maxima(p, 1, (lambda: lows(p, 1), lambda: gate(p)), wide)
                    dve.wait_ge(d_gate, p + 2)
                    finish(p, 0)
                    maxima(p, 2, (), wide)
                    finish(p, 1)
                    maxima(p, 3, () if final else (lambda: lows(p + 1, 0), lambda: None), wide)
                    finish(p, 2)
                    if not final:
                        maxima(p + 1, 0, (), wide)
                    else:
                        turn_inverses()
                    finish(p, 3)
                lows(0, 0)
                maxima(0, 0)
                for kv in range(KVH):
                    if kv == 0:
                        with dve.Fori(0, PAIRS // KVH) as p:
                            pair(p)
                    else:
                        pair(PAIRS - 2, True)
                        pair(PAIRS - 1, True, final=True)
                    if kv == 0:
                        dve.wait_ge(a_nd, STEPS + 2)
                        for z in range(2):
                            for half in range(2):
                                src = ND[z][:, 32 * half:32 * half + 32, :].rearrange("p g t -> p t g")
                                dst = NT[:, 2 * z + half].rearrange("p (a b) -> p a b", a=32)
                                dve.transpose(dst if z == 0 else dst.rearrange("p a b -> p b a"), src).then_inc(d_nt, 1)
                dve.wait_ge(d_inv, 8)

            @block.tensor
            def _(pe):
                pe.sem_inc(s_st, 32)
                pe.sem_inc(s_pv, 2)
                pe.sem_inc(s_g, 4)
                for c in range(TT):
                    if c >= 2:
                        pe.wait_ge(a_va, c + 1)
                    pe.transpose(PS[:, 4 + c % 2, 0:P], PJ[:, V0, c * P:(c + 1) * P], IDN[:, :]).then_inc(s_vtr, 1)
                pe.wait_ge(a_va, TT + 2)
                pe.wait_ge(a_va2, 1)
                pe.wait_ge(d_one, 1)
                pe.wait_ge(d_kl, KVH)

                def scores(kv, p, u, t, half):
                    c, first_wide = 4 * (4 * p + u) + t, 4 * (4 * (PAIRS // KVH) + 1)
                    wide = c >= first_wide
                    if half == 0:
                        pe.wait_ge(d_mx, c + 1 - (c > first_wide))
                        if c == first_wide + 1:
                            pe.wait_ge(a_nd, STEPS + 2)
                    q = slice((u % 2) * HALF + t * P, (u % 2) * HALF + (t + 1) * P)
                    for k, Q in enumerate((QH, QL)):
                        m = pe.matmul(PS[:, (2 * (t % 2) if wide else 0) + half], Q[:, u // 2, q], KHL[:, kv, half * HALF:(half + 1) * HALF],
                                      start=(k == 0), stop=(k == 1))
                    if half == 1:
                        m.then_inc(s_s, 1)

                def scores_t(kv, p, u, k):
                    pe.wait_ge(a_p, 8 * (4 * p + u) + k + 1)
                    o, q, key = PS[:, 4 + k % 2], slice((u % 2) * HALF, (u % 2 + 1) * HALF), slice(k * P, (k + 1) * P)
                    pe.matmul(o, KHL[:, kv, key], QH[:, u // 2, q], start=True, stop=False)
                    pe.matmul(o, KHL[:, kv, key], QL[:, u // 2, q], start=False, stop=False)
                    pe.matmul(o, ONE[:, :], DG[:, u % 2, :], start=False, stop=True).then_inc(s_st, 1)

                def products(p, u, k):
                    if k % 4 == 0:
                        pe.wait_ge(s_ld[k // 4], 48 * (4 * p + u + 1))
                    pe.wait_ge(a_nd, 4 * (4 * p + u) + k // 2 + 1)
                    for m in range(2):
                        last = pe.matmul(PS[:, 2 + k // 2 % 2, 2 * m * P:2 * (m + 1) * P], AI[:, k // 4, k % 4 + m, :],
                                         KX[:, k // 4, k % 4 + m].rearrange("p h n -> p (h n)"), start=True, stop=True)
                    last.then_inc(s_g, 1)

                def outputs(kv, p, u, k):
                    pe.wait_ge(a_p, 8 * (4 * p + u) + k + 3)
                    if k == 0:
                        pe.wait_ge(d_o, 4 * p + u + 1)
                    pe.matmul(PS[:, 6 + u % 2], VA[:, kv, k, :], PB[:, k % 2], start=(k == 0), stop=(k == TT - 1)).then_inc(s_pv, 1)

                pe.wait_ge(d_ql, 1)
                for t in range(4):
                    for half in range(2):
                        scores(0, 0, 0, t, half)
                for n in range(4 * PAIRS):
                    (p, u), (p1, u1) = divmod(n, 4), divmod(n + 1, 4)
                    kv, kv1 = p // (PAIRS // KVH), p1 // (PAIRS // KVH)
                    pe.wait_ge(d_dg, 4 * n + 4)
                    for k in range(TT):
                        scores_t(kv, p, u, k)
                        if kv == 0 and k % 2 == 0:
                            products(p, u, k)
                        if p1 < PAIRS:
                            if k == 0:
                                pe.wait_ge(d_ql, 2 * p1 + u1 // 2 + 1)
                            scores(kv1, p1, u1, k // 2, k % 2)
                        if k:
                            outputs(kv, p, u, k - 1)
                    outputs(kv, p, u, TT - 1)


def state_passes(nc, sem, PJ, HT, IDN, EMU, CACT, PS, consts, units, INV, WO, GACC, w_out, w_ada):
    with ExitStack() as st:
        sb = lambda name, shape, dt=F32: st.enter_context(nc.sbuf_tensor(name, shape, dt))
        Y = [HT[:, 4 * z:4 * z + 4, :].rearrange("p a b -> p (a b)").rearrange("p (m n) -> p m n", n=P) for z in range(2)]
        KX = sb("KX", [P, 4, 2, 2, P])
        AK = sb("AK", [P, 4, 2, P])
        VZ = sb("VZ", [P, 4, 2 * P])
        MSK = sb("MSK", [P, 2, 4, P])
        BD = sb("BD", [P, 4, 32])
        DG = sb("DG", [P, 2, P])
        EM2 = sb("EM2", [P, 2 * STEPS])
        SA, SB = sb("SA", [P, 2, 2, 2, P]), sb("SB", [P, 2, 2, 2, P])
        TOK, RH, ZT = sb("TOK", [P, 2, 2 * P]), sb("RH", [P, 2, 2 * P]), sb("ZT", [P, 2, 2 * P])
        W, WU = sb("W", [P, 2, 2 * P]), sb("WU", [P, 2, 2 * P])
        WT = sb("WT", [P, 2, P])
        RE, ATB, HB = sb("RE", [P, 2, P]), sb("ATB", [P, 2, P]), sb("HB", [P, 2, P])
        PX, PT = sb("PX", [P, 2, 2, P]), sb("PT", [P, 2, 2, P])
        WG = sb("WG", [P, 2, D])
        KEEP = sb("KEEP", [P, STEPS])

        s_wg, g_acc, s_wo = [sem(f"w_gate_loaded{u}") for u in range(2)], sem("gate_sums"), sem("w_out_loaded")
        s_cst, s_zero, s_ld = sem("consts5_loaded"), sem("s3_zeroed"), [sem(f"unit_loaded{r}") for r in range(4)]
        d_px, s_dg = sem("inverses_expanded"), sem("diag_ready")
        s_g1, s_g2, s_mv, s_zt, s_w, s_wu, s_rey, s_at, s_h = (sem(n) for n in (
            "pe_g1", "pe_g2", "pe_mv", "pe_zt", "pe_w", "pe_wu_plus_2", "pe_rey", "pe_at_b_plus_4", "pe_h_plus_1"))
        d_sa, d_sb, d_w, d_re, d_at, d_y, d_em = (sem(n) for n in ("sa_ready_plus_1", "sb_ready_plus_1", "w_ready", "re_ready_plus_4", "at_ready", "y_added_plus_1", "em2_ready"))
        a_tok, a_rh, a_zt, a_wu, a_y, a_h = (sem(n) for n in ("tok_ready", "rh_ready_plus_1", "zt_ready", "wu_ready", "y0_ready_plus_1", "h_ready_plus_1"))

        with nc.Block() as block:
            @block.sync
            def _(sp):
                sp.dma_start(MSK[:, :, :, :].rearrange("p z k n -> p (z k n)"), consts[:, CC["mask"]:CC["mask"] + 8 * P]).then_inc(s_cst, 16)
                sp.dma_start(BD[:, :, :].rearrange("p a b -> p (a b)"), consts[:, CC["bd"]:CC["bd"] + P]).then_inc(s_cst, 16)
                sp.dma_start(KEEP[:, :], consts[:, CC["keep"]:CC["keep"] + STEPS]).then_inc(s_cst, 16)
                sp.wait_ge(s_zero, 1)
                with sp.Fori(0, STEPS // 2) as i:
                    for r in range(4):
                        z, m, n = r % 2, 2 * i + r // 2, 4 * i + r + 1
                        sp.wait_ge(d_re, n)
                        sp.wait_ge(s_at, n)
                        for h in range(2):
                            rows = slice(h * HD, (h + 1) * HD)
                            sp.dma_start(KX[rows, r, h], units[z, ds(m, 1), rows, 0:2, :].rearrange("o p a n -> p (o a) n")).then_inc(s_ld[r], 16)
                        sp.dma_start(AK[:, r], units[z, ds(m, 1), :, 2:4, :].rearrange("o p a n -> p (o a) n")).then_inc(s_ld[r], 16)
                        sp.dma_start(VZ[:, r, HD:HD + P], units[z, ds(m, 1), :, 4, :].rearrange("o p n -> p (o n)")).then_inc(s_ld[r], 16)
                for k in range(KD):
                    sp.dma_start(WO[k], w_out[k * P:(k + 1) * P, :]).then_inc(s_wo, 16)
                sp.wait_ge(s_wo, 16 * KD)

            @block.gpsimd
            def _(pool):
                pool.memset(KX[:, :, :, :, :], 0.0)
                pool.memset(ATB[:, :, :], 0.0)
                pool.memset(HB[:, :, :], 0.0)
                pool.memset(VZ[:, :, :], 0.0)
                pool.drain().then_inc(s_zero, 1)
                for u in range(2):
                    pool.dma_start(WG[:, u], w_ada[u * P:(u + 1) * P, 2 * D:3 * D]).then_inc(s_wg[u], 16)
                for k in range(KD):
                    pool.wait_ge(s_wg[k % 2], 16 * (k // 2 + 1))
                    dst = WG[:, k % 2] if k else GACC[:, :]
                    pool.tensor_scalar(dst, WG[:, k % 2], CACT[:, k:k + 1], None, ALU.mult).then_inc(g_acc, 1)
                    pool.wait_ge(g_acc, max(2 * k, 1))
                    if k:
                        pool.tensor_tensor(GACC[:, :], GACC[:, :], WG[:, k % 2], ALU.add).then_inc(g_acc, 1)
                        pool.wait_ge(g_acc, 2 * k + 1)
                    if k + 2 < KD:
                        pool.dma_start(WG[:, k % 2], w_ada[(k + 2) * P:(k + 3) * P, 2 * D:3 * D]).then_inc(s_wg[k % 2], 16)

            @block.tensor
            def _(pe):
                pe.sem_inc(s_wu, 2)
                pe.sem_inc(s_at, 4)
                pe.sem_inc(s_h, 1)
                pe.wait_ge(s_zero, 1)
                pe.wait_ge(s_cst, 48)

                def g1(n, r, i):
                    pe.wait_ge(s_ld[r], 64 * (i + 1))
                    pe.wait_ge(d_sa, n + 1)
                    pe.matmul(PS[:, 0], AK[:, r, 0], KX[:, r].rearrange("p h a n -> p (h a n)"), start=True, stop=True).then_inc(s_g1, 1)

                def g2(n, r):
                    pe.wait_ge(d_sb, n + 1)
                    pe.matmul(PS[:, 1], AK[:, r, 1], KX[:, r].rearrange("p h a n -> p (h a n)"), start=True, stop=True).then_inc(s_g2, 1)

                def tokens(n, r):
                    z = r % 2
                    pe.wait_ge(s_dg, n + 1)
                    pe.wait_ge(a_rh, n + 1)
                    for k in range(2):
                        pe.matmul(PS[:, 2, 2 * P + k * P:3 * P + k * P], AK[:, r, k], DG[:, z, :], start=True, stop=True)
                    pe.matmul(PS[:, 2, 0:HD], KX[:, r, 0, 0], DG[:, z, 0:HD], start=True, stop=True)
                    pe.matmul(PS[:, 2, 3 * HD:4 * HD], KX[:, r, 1, 0], DG[:, z, HD:P], start=True, stop=True)

                def values(n, r):
                    z = r % 2
                    pe.wait_ge(d_sb, n + 2)
                    for h in range(2):
                        m = pe.matmul(PS[:, 2, (1 + h) * HD:(2 + h) * HD], SB[:, z, h, 0], VZ[:, r, (1 + h) * HD:(2 + h) * HD], start=True, stop=True)
                    m.then_inc(s_mv, 1)
                    pe.wait_ge(d_sa, n + 2)
                    pe.wait_ge(d_px, n + 1)
                    if not (isinstance(n, int) and n == 0):
                        pe.wait_ge(d_w, 3 * n - 1)
                    for h in range(2):
                        m = pe.matmul(PS[:, 3, h * P:(h + 1) * P], PX[:, z, h], SA[:, z, h, 0], start=True, stop=True)
                    m.then_inc(s_zt, 1)

                def round_(n, r, k):
                    z = r % 2
                    if k == 0:
                        pe.wait_ge(a_zt, n + 1)
                        pe.wait_ge(a_rh, n + 2)
                        src = RH[:, z]
                    else:
                        pe.wait_ge(d_w, 3 * n + k)
                        src = W[:, (k - 1) % 2]
                    for h in range(2):
                        m = pe.matmul(PS[:, 4 - k % 2, h * P:(h + 1) * P], ZT[:, z, h * P:(h + 1) * P], src[:, h * P:(h + 1) * P], start=True, stop=True)
                    m.then_inc(s_w, 1)

                def solve(n, r):
                    z = r % 2
                    pe.wait_ge(d_w, 3 * n + 3)
                    pe.wait_ge(d_y, n + 1)
                    for h in range(2):
                        m = pe.matmul(PS[:, 5, h * P:(h + 1) * P], PT[:, z, h], W[:, 0, h * P:(h + 1) * P], start=True, stop=True)
                    m.then_inc(s_wu, 1)

                def outputs(n, r):
                    z = r % 2
                    pe.wait_ge(a_wu, n + 1)
                    pe.wait_ge(d_re, n + 4)
                    pe.wait_ge(a_y, n + 1)
                    for h in range(2):
                        o = PS[:, 6, h * P:(h + 1) * P]
                        pe.matmul(o, WU[:, z, h * P:(h + 1) * P], SA[:, z, h, 1], start=True, stop=False)
                        m = pe.matmul(o, VZ[:, r, h * P:(h + 1) * P], SB[:, z, h, 1], start=False, stop=True)
                    m.then_inc(s_rey, 1)
                    pe.wait_ge(a_h, n + 1)
                    pe.matmul(PS[:, 7, 0:P], WT[:, z], TOK[:, z, 0:P], start=True, stop=True)
                    pe.matmul(PS[:, 7, P:2 * P], TOK[:, z, 0:P], WU[:, z, HD:HD + P], start=True, stop=False)
                    pe.matmul(PS[:, 7, P:2 * P], TOK[:, z, P:2 * P], VZ[:, r, HD:HD + P], start=False, stop=False).then_inc(s_at, 1)

                def state(n, r):
                    z = r % 2
                    pe.wait_ge(d_re, n + 5)
                    pe.wait_ge(a_wu, n + 1)
                    if not (isinstance(n, int) and n == 0):
                        pe.wait_ge(a_h, n)
                    pe.matmul(PS[:, 5, 0:P], HB[:, z], RE[:, z], start=True, stop=True)
                    pe.wait_ge(d_at, n + 1)
                    pe.matmul(PS[:, 7, P:2 * P], ATB[:, z], HB[:, z], start=False, stop=True).then_inc(s_h, 1)

                def early(n, r, i):
                    return [lambda: g1(n, r, i), lambda: g2(n, r), lambda: tokens(n, r), lambda: values(n, r)]

                def tile(n, r, nxt, prev):
                    round_(n, r, 0)
                    if nxt: nxt[0]()
                    round_(n, r, 1)
                    if nxt: nxt[1]()
                    if prev: state(*prev)
                    round_(n, r, 2)
                    if nxt: nxt[2]()
                    solve(n, r)
                    if nxt: nxt[3]()
                    outputs(n, r)

                for part in early(0, 0, 0):
                    part()
                LASTI = STEPS // 2 - 1
                tile(0, 0, early(1, 1, 0), None)
                for r in (1, 2):
                    tile(r, r, early(r + 1, r + 1, 0), (r - 1, r - 1))
                tile(3, 3, early(4, 0, 1), (2, 2))
                with pe.Fori(1, LASTI) as i:
                    for r in range(4):
                        n = 4 * i + r
                        nxt = early(n + 1, r + 1, i) if r < 3 else early(n + 1, 0, i + 1)
                        tile(n, r, nxt, (n - 1, (r - 1) % 4))
                for r in range(4):
                    n = 4 * LASTI + r
                    tile(n, r, early(n + 1, r + 1, LASTI) if r < 3 else None, (n - 1, (r - 1) % 4))
                state(4 * LASTI + 3, 3)

            @block.vector
            def _(dve):
                for s, v in ((d_sa, 1), (d_sb, 1), (d_re, 4), (d_y, 1)):
                    dve.sem_inc(s, v)
                dve.wait_ge(s_cst, 48)
                dve.wait_ge(s_zero, 1)
                dve.tensor_tensor(EM2[:, :], EMU[:, :], EMU[:, :], ALU.mult).then_inc(d_em, 1)
                dve.wait_ge(d_em, 1)
                bd = BD[:, :, :].unsqueeze(1).broadcast_to((P, 2, 4, 32))
                half_decay = lambda z, m, rows=slice(0, P): EMU[rows, ds(z * STEPS + m, 1)]

                def mask(S, bank, k, z):
                    dve.tensor_tensor(S[:, z], PS[:, bank].rearrange("p (h a n) -> p h a n", h=2, a=2),
                                      MSK[:, z, k:k + 2].unsqueeze(1).broadcast_to((P, 2, 2, P)), ALU.mult).then_inc(d_sa if k == 0 else d_sb, 1)

                def early(n, r, m):
                    z = r % 2

                    def a():
                        dve.wait_ge(s_g1, n + 1)
                        mask(SA, 0, 0, z)
                        dve.tensor_scalar(DG[:, z, :], IDN[:, :], half_decay(z, m), None, ALU.mult).then_inc(s_dg, 1)

                    def b():
                        dve.wait_ge(s_g2, n + 1)
                        mask(SB, 1, 2, z)

                    def c():
                        for k, dst in ((0, PX), (1, PT)):
                            last = dve.tensor_tensor(dst[:, z].rearrange("p h (b n) -> p h b n", b=4),
                                                     INV[k][z][:, ds(2 * m, 2), :].unsqueeze(2).broadcast_to((P, 2, 4, 32)), bd, ALU.mult)
                        last.then_inc(d_px, 1)
                    return [a, b, c]

                def add(n, r, k):
                    z = r % 2
                    dve.wait_ge(s_w, 3 * n + k + 1)
                    dve.tensor_tensor(W[:, k % 2], PS[:, 4 - k % 2, 0:2 * P], RH[:, z], ALU.add).then_inc(d_w, 1)

                def finish(n, r, m):
                    z = r % 2
                    dve.wait_ge(s_rey, n + 1)
                    for h in range(2):
                        rows = slice(h * HD, (h + 1) * HD)
                        last = dve.scalar_tensor_tensor(out=RE[rows, z], in0=KX[rows, r, h, 1], scalar=half_decay(z, m, rows),
                                                        in1=PS[rows, 6, h * P:(h + 1) * P], op0=ALU.mult, op1=ALU.add)
                    last.then_inc(d_re, 1)
                    dve.wait_ge(s_at, n + 5)
                    for h in range(2):
                        rows = slice(h * HD, (h + 1) * HD)
                        last = dve.scalar_tensor_tensor(out=ATB[rows, z, rows], in0=IDN[rows, rows], scalar=EM2[rows, ds(z * STEPS + m, 1)],
                                                        in1=PS[rows, 7, rows], op0=ALU.mult, op1=ALU.add)
                    last.then_inc(d_at, 1)

                def yadd(n, r, m):
                    z = r % 2
                    dve.wait_ge(s_h, n + 2)
                    dve.wait_ge(a_y, n + 2)
                    y = Y[z][:, ds(m, 1), :].rearrange("p o n -> p (o n)")
                    dve.tensor_tensor(y, PS[:, 5, 0:P], y, ALU.add).then_inc(d_y, 1)

                def tile(n, r, m, nxt, prev):
                    add(n, r, 0)
                    if nxt: nxt[2]()
                    add(n, r, 1)
                    if nxt: nxt[0]()
                    if prev: yadd(*prev)
                    add(n, r, 2)
                    if nxt: nxt[1]()
                    finish(n, r, m)
                drive(dve, early, tile, lambda n, r, m: yadd(n, r, m))

            @block.scalar
            def _(act):
                for s in (a_rh, a_y, a_h):
                    act.sem_inc(s, 1)
                act.wait_ge(s_cst, 48)

                def early(n, r, m):
                    z = r % 2

                    def a():
                        act.wait_ge(s_mv, n + 1)
                        act.activation(TOK[:, z], PS[:, 2, 2 * P:4 * P], ACT.Copy).then_inc(a_tok, 1)
                        act.activation(RH[:, z], PS[:, 2, 0:2 * P], ACT.Copy).then_inc(a_rh, 1)
                        act.wait_ge(s_zt, n + 1)
                        act.activation(ZT[:, z], PS[:, 3, 0:2 * P], ACT.Copy).then_inc(a_zt, 1)
                    return [a]

                def state(n, r, m):
                    z = r % 2
                    act.wait_ge(s_cst, 48)
                    act.wait_ge(s_h, n + 2)
                    for h in range(2):
                        rows = slice(h * HD, (h + 1) * HD)
                        last = act.activation(HB[rows, z, rows], PS[rows, 7, P + h * HD:P + (h + 1) * HD], ACT.Copy, scale=KEEP[rows, ds(m, 1)])
                    last.then_inc(a_h, 1)

                def tile(n, r, m, nxt, prev):
                    z = r % 2
                    if prev: state(*prev)
                    act.wait_ge(s_wu, n + 3)
                    act.activation(WU[:, z], PS[:, 5, 0:2 * P], ACT.Copy)
                    act.activation(WT[:, z].rearrange("p (a b) -> p a b", b=HD),
                                   PS[:, 5, 0:2 * P].rearrange("p (a b) -> p a b", b=HD)[:, 0:4:3, :], ACT.Copy).then_inc(a_wu, 1)
                    if nxt: nxt[0]()
                    act.wait_ge(d_re, n + 5)
                    act.activation(Y[z][0:HD, ds(m, 1), :].rearrange("p o n -> p (o n)"), PS[HD:P, 6, 0:P], ACT.Copy)
                    act.activation(Y[z][HD:P, ds(m, 1), :].rearrange("p o n -> p (o n)"), PS[0:HD, 6, P:2 * P], ACT.Copy).then_inc(a_y, 1)
                drive(act, early, tile, lambda n, r, m: state(n, r, m))


def finish_layer(nc, sem, PJ, HT, PS, prm, WO, GACC, x, b_gate, g_post, consts, out):
    with ExitStack() as st:
        sb = lambda name, shape, dt=F32: st.enter_context(nc.sbuf_tensor(name, shape, dt))
        ROWS = sb("ROWS6", [P, 9, 32])
        SPR = sb("SPR6", [P, 9, P])
        BLK = sb("BLK6", [P, P])
        ONES = sb("ONES6", [P, P])
        RST = sb("RST6", [P, T])
        TG = sb("TG6", [P, 2, T])
        G = sb("G", [P, D])
        GP = sb("GP", [P, D])
        XT = sb("XT", [P, 2, D])
        M = sb("M", [P, 2, D])
        SQ = sb("SQ6", [P, 2, D])
        SS, RS = sb("SS6", [P, 2]), sb("RS6", [P, 2])
        s_cst, s_one, s_gb = sem("consts6_loaded"), sem("ones6_ready"), sem("gate_params_loaded")
        s_gs, d_g = sem("gate_summed"), sem("gate6_ready")
        d_sum, s_mean, d_c, a_sq, s_rows = sem("directions_summed"), sem("means_ready"), sem("centred"), sem("squares6_ready"), sem("variances_summed")
        d_var, a_rst, s_spr, d_gn = sem("variance_inverse"), sem("rstd6_ready"), sem("rstd_spread"), sem("group_normed")
        a_tg, d_tg, d_y, d_mix, s_dve = sem("tanh_gate"), sem("silu_gate"), sem("bonus_added"), sem("mixed_ready"), sem("dve_chain6")
        s_x, s_out = [sem(f"x6_loaded{u}") for u in range(2)], [sem(f"out_stored{u}_plus_16") for u in range(2)]
        s_mm, a_ss, d_v, a_rs, d_m, d_o = sem("tile_projected"), sem("tile_squares"), sem("tile_inverse"), sem("tile_rstd"), sem("tile_scaled"), sem("tile_ready")
        banks = lambda b: PS[:, b:b + 2].rearrange("p a b -> p (a b)")
        MIXED = [GA0 + j for j in range(PAIRS)] + [GR0 + j for j in range(PAIRS)]
        chunks = lambda a: a.rearrange("p (c n) -> p c n", c=TT)
        tokens = lambda a, t: a[ds(t * P, P), :]

        with nc.Block() as block:
            @block.sync
            def _(sp):
                for dst, name, w, rows in ((BLK[:, :], "blocks", P, P), (ROWS[:, :, :].rearrange("p a b -> p (a b)"), "rows", 9 * 32, P),
                                           (SPR[:, :, :].rearrange("p a b -> p (a b)"), "spread", 9 * P, P)):
                    sp.dma_start(dst, consts[0:rows, CC[name]:CC[name] + w]).then_inc(s_cst, 16)
                sp.dma_start(G[:, :], b_gate.broadcast_to((P, D))).then_inc(s_gb, 16)
                sp.dma_start(GP[:, :], g_post.broadcast_to((P, D))).then_inc(s_gb, 16)
                for u in range(2):
                    sp.sem_inc(s_out[u], 16)
                with sp.Fori(0, TT // 2) as i:
                    for u in range(2):
                        sp.wait_ge(s_out[u], 16 * i + 16)
                        sp.dma_start(XT[:, u], tokens(x, 2 * i + u)).then_inc(s_x[u], 16)
                    for u in range(2):
                        sp.wait_ge(d_o, 2 * i + u + 1)
                        sp.dma_start(tokens(out, 2 * i + u), XT[:, u]).then_inc(s_out[u], 16)
                for u in range(2):
                    sp.wait_ge(s_out[u], 16 * (TT // 2) + 16)

            @block.gpsimd
            def _(pool):
                pool.memset(ONES[:, :], 1.0).then_inc(s_one, 1)
                pool.memset(RST[:, :], 0.0).then_inc(s_one, 1)

            @block.scalar
            def _(act):
                for j in range(PAIRS):
                    if j >= 2:
                        act.wait_ge(d_tg, j - 1)
                    act.activation(TG[:, j % 2], PJ[:, GR0 + j, :], ACT.Tanh, scale=0.5).then_inc(a_tg, 1)
                    act.wait_ge(d_c, j + 1)
                    act.activation(HT[:, PAIRS + j], HT[:, j], ACT.Square, scale=HD ** -0.5).then_inc(a_sq, 1)
                act.wait_ge(d_var, 1)
                act.activation(RST[0:32, :], RST[0:32, :], ACT.Sqrt).then_inc(a_rst, 1)
                with act.Fori(0, TT // 2) as i:
                    for u in range(2):
                        act.wait_ge(s_mm, 2 * i + u + 1)
                        act.activation(SQ[:, u], banks(4 + 2 * u), ACT.Square, scale=D ** -0.5, accum_out=SS[:, u:u + 1]).then_inc(a_ss, 1)
                        act.wait_ge(d_v, 2 * i + u + 1)
                        act.activation(RS[:, u:u + 1], SS[:, u:u + 1], ACT.Sqrt).then_inc(a_rs, 1)

            @block.vector
            def _(dve):
                for j in range(PAIRS):
                    dve.tensor_tensor(chunks(HT[:, j]), chunks(HT[:, j]), chunks(HT[:, PAIRS + j])[:, ORDER[1], :], ALU.add).then_inc(d_sum, 1)
                for j in range(PAIRS):
                    dve.wait_ge(d_sum, j + 1)
                    dve.wait_ge(s_mean, j + 1)
                    dve.scalar_tensor_tensor(out=HT[:, j], in0=banks(0), scalar=-1.0 / HD, in1=HT[:, j], op0=ALU.mult, op1=ALU.add).then_inc(d_c, 1)
                    dve.wait_ge(a_tg, j + 1)
                    dve.scalar_tensor_tensor(out=PJ[:, GR0 + j, :], in0=TG[:, j % 2], scalar=1.0, in1=PJ[:, GR0 + j, :],
                                             op0=ALU.add, op1=ALU.mult).then_inc(d_tg, 1)
                dve.wait_ge(s_one, 2)
                dve.wait_ge(s_rows, 1)
                dve.tensor_scalar(RST[0:32, :], PS[0:32, 2:4].rearrange("p a b -> p (a b)"), GN_EPS, None, ALU.add).then_inc(s_dve, 1)
                dve.wait_ge(s_dve, 1)
                dve.reciprocal(RST[0:32, :], RST[0:32, :]).then_inc(d_var, 1)
                for j in range(PAIRS):
                    dve.wait_ge(s_spr, j + 1)
                    dve.scalar_tensor_tensor(out=HT[:, j], in0=HT[:, j], scalar=prm("gn_w", j), in1=banks(2 * (j % 2)),
                                             op0=ALU.mult, op1=ALU.mult).then_inc(d_gn, 1)
                    dve.wait_ge(d_gn, j + 1)
                    dve.scalar_tensor_tensor(out=HT[:, j], in0=HT[:, j], scalar=prm("gn_b", j), in1=PJ[:, RV0 + j, :],
                                             op0=ALU.add, op1=ALU.add).then_inc(d_y, 1)
                    dve.wait_ge(d_y, j + 1)
                    dve.wait_ge(d_tg, j + 1)
                    dve.scalar_tensor_tensor(out=PJ[:, GR0 + j, :], in0=PJ[:, GR0 + j, :], scalar=0.5, in1=HT[:, j],
                                             op0=ALU.mult, op1=ALU.mult).then_inc(d_mix, 1)
                dve.wait_ge(s_gb, 32)
                dve.wait_ge(s_gs, 1)
                dve.tensor_tensor(G[:, :], banks(0), G[:, :], ALU.add).then_inc(d_g, 1)
                dve.wait_ge(d_g, 1)
                dve.tensor_tensor(G[:, :], G[:, :], GP[:, :], ALU.mult).then_inc(d_g, 1)
                dve.wait_ge(d_g, 2)
                with dve.Fori(0, TT // 2) as i:
                    for u in range(2):
                        n = 2 * i + u + 1
                        dve.wait_ge(a_ss, n)
                        dve.tensor_scalar(SS[:, u:u + 1], SS[:, u:u + 1], NORM_EPS, None, ALU.add).then_inc(s_dve, 1)
                        dve.wait_ge(s_dve, n + 1)
                        dve.reciprocal(SS[:, u:u + 1], SS[:, u:u + 1]).then_inc(d_v, 1)
                        dve.wait_ge(a_rs, n)
                        dve.scalar_tensor_tensor(out=M[:, u], in0=banks(4 + 2 * u), scalar=RS[:, u:u + 1], in1=G[:, :],
                                                 op0=ALU.mult, op1=ALU.mult).then_inc(d_m, 1)
                        dve.wait_ge(d_m, n)
                        dve.wait_ge(s_x[u], 16 * (i + 1))
                        dve.tensor_tensor(XT[:, u], XT[:, u], M[:, u], ALU.add).then_inc(d_o, 1)

            @block.tensor
            def _(pe):
                def project(t, first, last):
                    for k in range(first, last):
                        for half in range(2):
                            m = pe.matmul(PS[:, 4 + 2 * (t % 2) + half], PJ[:, MIXED[k], t * P:(t + 1) * P],
                                          WO[k][:, half * HALF:(half + 1) * HALF], start=(k == 0), stop=(k == KD - 1))
                    return m

                def spread(lhs, rhs, bank):
                    for half in range(2):
                        m = pe.matmul(PS[0:lhs.shape[1], bank + half], lhs, rhs[:, half * HALF:(half + 1) * HALF], start=True, stop=True)
                    return m
                pe.wait_ge(s_cst, 48)
                pe.wait_ge(s_one, 2)
                for j in range(PAIRS):
                    pe.wait_ge(d_sum, j + 1)
                    if j:
                        pe.wait_ge(d_c, j)
                    spread(BLK[:, :], HT[:, j], 0).then_inc(s_mean, 1)
                    project(j // 2, 2 * (j % 2), 2 * (j % 2) + 2)
                for j in range(PAIRS):
                    pe.wait_ge(a_sq, j + 1)
                    for half in range(2):
                        m = pe.matmul(PS[0:32, 2 + half], ROWS[:, j, :], HT[:, PAIRS + j, half * HALF:(half + 1) * HALF],
                                      start=(j == 0), stop=(j == PAIRS - 1))
                m.then_inc(s_rows, 1)
                pe.wait_ge(a_rst, 1)
                for j in range(PAIRS):
                    if j >= 2:
                        pe.wait_ge(d_gn, j - 1)
                    spread(SPR[:, j, :], RST[:, :], 2 * (j % 2)).then_inc(s_spr, 1)
                pe.wait_ge(d_gn, 3)
                spread(ONES[:, :], GACC[:, :], 0).then_inc(s_gs, 1)
                for t in range(TT):
                    if t < 2:
                        for j in range(PAIRS):
                            pe.wait_ge(d_mix, j + 1)
                            m = project(t, PAIRS + j, PAIRS + j + 1)
                    else:
                        pe.wait_ge(d_m, t - 1)
                        m = project(t, 0, KD)
                    m.then_inc(s_mm, 1)


def drive(eng, early, tile, last):
    chunk = lambda i, r: 2 * i + r // 2
    for part in early(0, 0, 0):
        part()
    end = STEPS // 2 - 1

    def four(i, first, final):
        for r in range(4):
            n = 4 * i + r
            nxt = early(n + 1, r + 1, chunk(i, r + 1)) if r < 3 else None if final else early(n + 1, 0, chunk(i + 1, 0))
            prev = None if first and r == 0 else (n - 1, (r - 1) % 4, chunk(i, r - 1) if r else chunk(i - 1, 3))
            tile(n, r, chunk(i, r), nxt, prev)
    four(0, True, False)
    with eng.Fori(1, end) as i:
        four(i, False, False)
    four(end, False, True)
    last(4 * end + 3, 3, chunk(end, 3))


def _columns(v):
    return v.reshape(-1, P).T


def kernel(x, c, w_ada, b_ada, g_pre, w_in, q_norm_g, k_norm_g, shift_taps, w_up, w0, a_up, a0, k_k, k_a, r_k,
           gn_w, gn_b, w_out, g_post):
    import numpy as np
    import concourse.bacc as bacc
    from concourse.bass_utils import run_bass_kernel_spmd

    f = lambda a: np.asarray(a)
    two = lambda v: np.concatenate([v, v])
    parts = {"c": _columns(f(c)[0]), "b_shift": _columns(f(b_ada)[0, :D]), "b_scale": _columns(f(b_ada)[0, D:2 * D]),
             "g_pre": _columns(f(g_pre)[0]),
             "taps": np.concatenate([_columns(f(shift_taps)[0, i]) for i in range(3)], 1),
             "w0": _columns(f(w0)[0].reshape(-1)), "a0": _columns(f(a0)[0].reshape(-1)),
             "k_k": _columns(f(k_k)[0]), "k_a": _columns(f(k_a)[0]), "r_k": _columns(f(r_k)[0].reshape(-1)),
             "gn_w": _columns(f(gn_w)[0]), "gn_b": _columns(f(gn_b)[0]),
             "q_g": two(f(q_norm_g)[0])[:, None], "k_g": two(f(k_norm_g)[0])[:, None]}
    params = np.zeros((P, NPC), np.float32)
    for name, a in parts.items():
        params[:, PC[name]:PC[name] + a.shape[1]] = a
    consts = shape_constants()
    arrays = {"x": f(x)[0], "w_ada": f(w_ada)[0], "w_in": f(w_in)[0], "w_up": f(w_up)[0], "a_up": f(a_up)[0],
              "w_out": f(w_out)[0], "b_gate": f(b_ada)[:, 2 * D:], "g_post": f(g_post), "params": params, "consts": consts}
    arrays = {n: np.ascontiguousarray(a) for n, a in arrays.items()}
    nc = bacc.Bacc("TRN2", target_bir_lowering=False, num_devices=1)
    aps = {n: nc.dram_tensor(f"in_{n}", a.shape, F32, kind="ExternalInput").ap() for n, a in arrays.items()}
    aps["out"] = nc.dram_tensor("out_x", (T, D), F32, kind="ExternalOutput").ap()
    hybrid_layer(nc, **aps)
    r = run_bass_kernel_spmd(nc, [{f"in_{n}": a for n, a in arrays.items()}], core_ids=[0])
    return r.results[0]["out_x"].reshape(1, T, D)


def shape_constants():
    import numpy as np

    k = np.zeros((P, NCC), np.float32)
    i = np.arange(P)
    put = lambda name, a: k[:, CC[name]:CC[name] + a.shape[1]].__setitem__(slice(None), a)
    put("ident", np.eye(P, dtype=np.float32))
    put("blocks", (i[:, None] // HD == i[None, :] // HD).astype(np.float32))
    rot = np.zeros((P, P), np.float32)
    for t in range(P):
        first = t % 32 < 16
        rot[t + 16 if first else t - 16, t] = -1.0 if first else 1.0
    put("rot", rot)
    s, t = i[:, None], i[None, :]
    m = np.zeros((P, 2, 4, P), np.float32)
    for z in range(2):
        a, b = (s, t) if z == 0 else (t, s)
        m[:, z, 0] = (a < b) & (s // 32 != t // 32)
        m[:, z, 1] = m[:, z, 3] = a <= b
        m[:, z, 2] = a < b
    put("mask", m.reshape(P, -1))
    put("bd", (i[:, None] // 32 == i[None, :] // 32).astype(np.float32))
    put("keep", np.broadcast_to((np.arange(STEPS) % TT != TT - 1).astype(np.float32), (P, STEPS)))
    n_freq = HD // 4
    inv = np.float32(10000.0) ** (-np.arange(n_freq, dtype=np.float32) / np.float32(n_freq))
    pos = np.arange(T)
    grid_w = 64
    at = np.where((i % HD < 32)[:, None], (pos // grid_w)[None, :], (pos % grid_w)[None, :]).astype(np.float32)
    ang = at * inv[i % 16][:, None].astype(np.float32)
    put("cos", np.cos(ang).astype(np.float32))
    put("sin", np.sin(ang).astype(np.float32))
    put("start", np.broadcast_to((pos % P != 0).astype(np.float32), (P, T)))
    rows = np.zeros((P, 9, 32), np.float32)
    spread = np.zeros((P, 9, P), np.float32)
    for j in range(9):
        for h in range(2):
            rows[h * HD:(h + 1) * HD, j, 2 * j + h] = 1.0
            spread[2 * j + h, j, h * HD:(h + 1) * HD] = 1.0
    put("rows", rows.reshape(P, -1))
    put("spread", spread.reshape(P, -1))
    put("eps", np.where(i < 2 * PAIRS, L2_EPS, NORM_EPS)[:, None].astype(np.float32))
    return k
```
